# Optimizing a Trainium2 kernel written in Bass

```python
import jax, jax.numpy as jnp
from jax import lax
import numpy as np

D_MODEL = 1024
BATCH = 1
SEQ = 512
DEPTH = 1

SC_WIDTH = D_MODEL // 2
CONV_W = 3
N_HEADS = 8
HEAD_DIM = D_MODEL // 16
ATTN_WIDTH = N_HEADS * HEAD_DIM
IDX_HEADS = 8
IDX_DIM = 32
TOPK_MAX = 256
QBLOCK = 128
MEM_TOKENS = 256
MEM_HEADS = 4
MEM_HEAD_DIM = D_MODEL // 8
MEM_WIDTH = MEM_HEADS * MEM_HEAD_DIM
N_BRANCH = 3
D_FF = ((8 * D_MODEL // 3 + 127) // 128) * 128
EPS = 1e-6
IN_SPLITS = (SC_WIDTH, SC_WIDTH, SC_WIDTH,
             ATTN_WIDTH, ATTN_WIDTH, ATTN_WIDTH,
             IDX_HEADS * IDX_DIM, IDX_DIM, IDX_HEADS,
             MEM_WIDTH, N_BRANCH * D_MODEL)
IN_WIDTH = sum(IN_SPLITS)

kernel_name = 'hybrid_shortconv_dsa_memxattn_convffn'

def rmsnorm(x, g):
    xf = x.astype(jnp.float32)
    y = xf * lax.rsqrt(jnp.mean(xf * xf, axis=-1, keepdims=True) + EPS)
    return (y * g.astype(jnp.float32)).astype(x.dtype)

def causal_dwconv(u, w):
    return lax.conv_general_dilated(
        u, w[:, None, :].astype(u.dtype), window_strides=(1,),
        padding=[(w.shape[0] - 1, 0)],
        dimension_numbers=('NWC', 'WIO', 'NWC'),
        feature_group_count=u.shape[-1])

def alibi_slopes(n_heads):
    return 2.0 ** (-8.0 * jnp.arange(1, n_heads + 1, dtype=jnp.float32) / n_heads)

def dsa_attention(q, k, v, qi, ki, wi):
    B, T = q.shape[0], q.shape[1]
    nblk = T // QBLOCK
    k_sel = min(TOPK_MAX, T // 4)
    slopes = alibi_slopes(N_HEADS)
    scale = HEAD_DIM ** -0.5
    key_pos = jnp.arange(T, dtype=jnp.int32)
    b_ids = jnp.repeat(jnp.arange(B, dtype=jnp.int32), nblk)
    starts = jnp.tile(jnp.arange(nblk, dtype=jnp.int32) * QBLOCK, B)

    def blocks(a):
        return a.reshape((B * nblk, QBLOCK) + a.shape[2:])

    def one_block(args):
        q_blk, qi_blk, wi_blk, b, start = args
        t = start + jnp.arange(QBLOCK, dtype=jnp.int32)
        idx_logits = jnp.einsum('qhd,sd->qhs', qi_blk, ki[b])
        score = jnp.einsum('qh,qhs->qs', wi_blk, jax.nn.relu(idx_logits)).astype(jnp.float32)
        score = jnp.where(key_pos[None, :] <= t[:, None], score, -jnp.inf)
        _, sel = lax.top_k(score, k_sel)
        valid = sel <= t[:, None]
        k_g = jnp.take(k[b], sel, axis=0)
        v_g = jnp.take(v[b], sel, axis=0)
        logits = jnp.einsum('qhd,qkhd->qhk', q_blk, k_g).astype(jnp.float32) * scale
        dist = (t[:, None] - sel).astype(jnp.float32)
        logits = logits - slopes[None, :, None] * dist[:, None, :]
        logits = jnp.where(valid[:, None, :], logits, -jnp.inf)
        p = jax.nn.softmax(logits, axis=-1).astype(v.dtype)
        return jnp.einsum('qhk,qkhd->qhd', p, v_g)

    out = lax.map(one_block, (blocks(q), blocks(qi), blocks(wi), b_ids, starts))
    return out.reshape(B, T, ATTN_WIDTH)

def hybrid_layer(x, mem, g_mix, w_in, conv_a_w, w_a_out, q_norm_g, k_norm_g, w_b_out,
                 g_mem, w_mem_kv, mq_norm_g, mk_norm_g, w_m_out, w_o,
                 g_ffn, w_up, conv_f_w, w_down):
    B, T, D = x.shape
    M = mem.shape[1]
    xn = rmsnorm(x, g_mix)
    proj = xn @ w_in
    (b_a, c_a, h_a, q, k, v, qi, ki, wi, qm, gate_logits) = jnp.split(
        proj, np.cumsum(IN_SPLITS)[:-1].tolist(), axis=-1)

    y_a = (b_a * causal_dwconv(c_a * h_a, conv_a_w)) @ w_a_out

    q = rmsnorm(q.reshape(B, T, N_HEADS, HEAD_DIM), q_norm_g)
    k = rmsnorm(k.reshape(B, T, N_HEADS, HEAD_DIM), k_norm_g)
    v = v.reshape(B, T, N_HEADS, HEAD_DIM)
    qi = qi.reshape(B, T, IDX_HEADS, IDX_DIM)
    y_b = dsa_attention(q, k, v, qi, ki, wi) @ w_b_out

    memn = rmsnorm(mem, g_mem)
    km, vm = jnp.split(memn @ w_mem_kv, 2, axis=-1)
    qm = rmsnorm(qm.reshape(B, T, MEM_HEADS, MEM_HEAD_DIM), mq_norm_g)
    km = rmsnorm(km.reshape(B, M, MEM_HEADS, MEM_HEAD_DIM), mk_norm_g)
    vm = vm.reshape(B, M, MEM_HEADS, MEM_HEAD_DIM)
    m_logits = jnp.einsum('bthd,bmhd->bhtm', qm, km).astype(jnp.float32) * (MEM_HEAD_DIM ** -0.5)
    m_p = jax.nn.softmax(m_logits, axis=-1).astype(vm.dtype)
    y_m = jnp.einsum('bhtm,bmhd->bthd', m_p, vm).reshape(B, T, MEM_WIDTH) @ w_m_out

    gates = jax.nn.sigmoid(gate_logits.astype(jnp.float32)).astype(x.dtype).reshape(B, T, N_BRANCH, D)
    merged = gates[:, :, 0] * y_a + gates[:, :, 1] * y_b + gates[:, :, 2] * y_m
    x = x + merged @ w_o

    up = causal_dwconv(rmsnorm(x, g_ffn) @ w_up, conv_f_w)
    gate, val = jnp.split(up, 2, axis=-1)
    return x + (jax.nn.silu(gate) * val) @ w_down

def setup_inputs(seed: int = 0) -> dict:
    key = jax.random.key(seed)
    ks = jax.random.split(key, 20)
    f32 = jnp.float32

    def nrm(k, shape, fan_in):
        return jax.random.normal(k, shape, f32) * (fan_in ** -0.5)

    def gain(k, n):
        return 1.0 + 0.02 * jax.random.normal(k, (DEPTH, n), f32)

    return {
        'x': jax.random.normal(ks[0], (BATCH, SEQ, D_MODEL), f32),
        'mem': jax.random.normal(ks[1], (BATCH, MEM_TOKENS, D_MODEL), f32),
        'g_mix': gain(ks[2], D_MODEL),
        'w_in': nrm(ks[3], (DEPTH, D_MODEL, IN_WIDTH), D_MODEL),
        'conv_a_w': nrm(ks[4], (DEPTH, CONV_W, SC_WIDTH), CONV_W),
        'w_a_out': nrm(ks[5], (DEPTH, SC_WIDTH, D_MODEL), SC_WIDTH),
        'q_norm_g': gain(ks[6], HEAD_DIM),
        'k_norm_g': gain(ks[7], HEAD_DIM),
        'w_b_out': nrm(ks[8], (DEPTH, ATTN_WIDTH, D_MODEL), ATTN_WIDTH),
        'g_mem': gain(ks[9], D_MODEL),
        'w_mem_kv': nrm(ks[10], (DEPTH, D_MODEL, 2 * MEM_WIDTH), D_MODEL),
        'mq_norm_g': gain(ks[11], MEM_HEAD_DIM),
        'mk_norm_g': gain(ks[12], MEM_HEAD_DIM),
        'w_m_out': nrm(ks[13], (DEPTH, MEM_WIDTH, D_MODEL), MEM_WIDTH),
        'w_o': nrm(ks[14], (DEPTH, D_MODEL, D_MODEL), D_MODEL),
        'g_ffn': gain(ks[15], D_MODEL),
        'w_up': nrm(ks[16], (DEPTH, D_MODEL, 2 * D_FF), D_MODEL),
        'conv_f_w': nrm(ks[17], (DEPTH, CONV_W, 2 * D_FF), CONV_W),
        'w_down': nrm(ks[18], (DEPTH, D_FF, D_MODEL), D_FF),
    }

def reference(x, mem, g_mix, w_in, conv_a_w, w_a_out, q_norm_g, k_norm_g, w_b_out,
              g_mem, w_mem_kv, mq_norm_g, mk_norm_g, w_m_out, w_o,
              g_ffn, w_up, conv_f_w, w_down):
    for l in range(DEPTH):
        x = hybrid_layer(x, mem, g_mix[l], w_in[l], conv_a_w[l], w_a_out[l],
                         q_norm_g[l], k_norm_g[l], w_b_out[l], g_mem[l], w_mem_kv[l],
                         mq_norm_g[l], mk_norm_g[l], w_m_out[l], w_o[l],
                         g_ffn[l], w_up[l], conv_f_w[l], w_down[l])
    return x


_drawn_inputs = setup_inputs


def setup_inputs(seed=0):
    import zlib

    import numpy as np

    out = dict(_drawn_inputs(seed))
    spreads = {}
    factors = {'q_norm_g': 8.0,
     'k_norm_g': 8.0,
     'g_mem': 8.0,
     'mq_norm_g': 8.0,
     'mk_norm_g': 8.0,
     'g_ffn': 4.297}
    for name, (base, spread) in spreads.items():
        noise = np.random.default_rng([zlib.crc32(name.encode()), seed]).standard_normal(out[name].shape)
        drawn = base * np.exp(spread * noise) if base else spread * noise
        out[name] = __import__('jax').numpy.asarray(drawn.astype(out[name].dtype))
    for name, factor in factors.items():
        out[name] = (out[name] * factor).astype(out[name].dtype)
    return out
```

```python
from contextlib import ExitStack

import concourse.bass as bass
from concourse import mybir

F32 = mybir.dt.float32
F32R = mybir.dt.float32r
ALU = mybir.AluOpType
ACT = mybir.ActivationFunctionType
AX = mybir.AxisListType

P = 128
D = 1024
T = 512
M = 256
KD = D // P
TB = T // P
MB = M // P
SC = D // 2
AW = 512
HD = 64
IH, ID = 8, 32
MHD = 128
FF = 2816
FT = FF // P
TOPK = 128
EPS = 1e-6
PANEL = 2048
COLS = PANEL // KD
FILL = -3.0e38
FAR = 1e32

C_B, C_C, C_H, C_Q, C_K, C_V = (i * 512 for i in range(6))
C_KI = C_V + 512 + IH * ID
C_QI = C_V + 512
C_QM = C_KI + ID + IH
C_GATE = C_QM + 512


def hybrid_layer(nc, x, mem, g_mix, w_in, conv_a_w, w_a_out, q_norm_g, k_norm_g, w_b_out, g_mem, w_mem_kv,
                 mq_norm_g, mk_norm_g, w_m_out, w_o, g_ffn, w_up, conv_f_w, w_down, out):
    kxn = lambda w: w[0].rearrange("(k p) n -> p k n", p=P)
    win, wkv, wup, wdown, wo = kxn(w_in), kxn(w_mem_kv), kxn(w_up), kxn(w_down), kxn(w_o)
    wide = lambda w, c: w[:, :, c:c + COLS]
    panels = [("ki", 0, win[:, :, C_KI:C_KI + ID + IH]), ("qi", 0, wide(win, C_QI))]
    for kind, base, w in (("k", C_K, win), ("q", C_Q, win), ("v", C_V, win), ("qm", C_QM, win),
                          ("km", 0, wkv), ("vm", AW, wkv)):
        panels += [(kind, half, wide(w, base + half * COLS)) for half in range(2)]
    for half in range(2):
        panels += [(kind, half, wide(win, base + half * COLS)) for kind, base in (("c", C_C), ("h", C_H), ("b", C_B))]
    BRANCHES = (("a", 0, kxn(w_a_out)), ("m", 2, kxn(w_m_out)), ("y", 1, kxn(w_b_out)))
    for name, gate, w in BRANCHES:
        gates = [("g" + name, i, wide(win, C_GATE + gate * D + i * COLS)) for i in range(4)]
        outs = [("w" + name, i, w[:, :, i * 512:(i + 1) * 512]) for i in range(2)]
        panels += gates + outs if name == "y" else gates[:2] + outs[:1] + gates[2:] + outs[1:]
    for half in range(2):
        for kh in range(2):
            panels.append(("wo", 2 * half + kh, wo[:, 4 * kh:4 * kh + 4, half * 512:half * 512 + 512]))
    N_HEAD = len(panels)
    N_UP = 2 * FT * P // COLS
    N_DOWN = FT // 2
    UP0, DOWN0 = N_HEAD, N_HEAD + N_UP
    assert UP0 % 2 == 0 and DOWN0 % 2 == 0

    bank_uses = {}
    last_reader = []

    def uses(key, n, reader):
        bank_uses[key] = len(last_reader)
        last_reader.extend([reader] * n)

    uses(("xT", 0), 2 * TB, "dve")
    per_panel = {"ki": (1, "act"), "qi": (2, "act"), "k": (2, "dve"), "q": (2, "dve"), "v": (2, "act"),
                 "qm": (2, "dve"), "km": (1, "dve"), "vm": (1, "act"), "c": (2, "act"), "h": (2, "dve"),
                 "b": (2, "dve"), "g": (2, "act"), "w": (4, "dve")}
    for kind, half, _ in panels:
        if kind == "qm" and half == 0:
            uses(("memT", 0), 2 * MB, "dve")
        if kind == "wo":
            if half % 2 == 0:
                uses((kind, half), 4, "dve")
        else:
            uses((kind, half), *per_panel[kind if kind in per_panel else kind[0]])
    uses(("x2T", 0), 2 * TB, "dve")
    N_USES = len(last_reader)
    assert last_reader[-4:] == ["dve"] * 4
    DVE_USES = last_reader.count("dve")

    IDX = [(b, h) for b in range(1, TB) for h in range(IH)]
    UNITS = [("m", h, b) for h in range(4) for b in range(TB)]
    UNITS += [("s", h, b) for hp in range(4) for h in (2 * hp, 2 * hp + 1) for b in range(TB)]
    N_UNITS = len(UNITS)
    score_reader = ["act"] * len(IDX) + ["exp" if u[0] == "m" else "dve" for u in UNITS]
    N_CHAINS = 14
    PT0 = 1 + N_CHAINS
    keys = lambda kind, b: M if kind == "m" else (b + 1) * P
    group_end = {u: g for g, u in enumerate([3, 7, 11, 15, 23, 31, 39, 47])}
    group_start = {0: 0, 4: 1, 8: 2, 12: 3, 16: 4, 24: 5, 32: 6, 40: 7}

    slots_at, s = {}, 0
    for kind, half, _ in panels:
        if kind in ("c", "h", "b", "ga", "wa", "gm", "wm"):
            for t in range(4 if kind[0] == "w" else 2):
                n = 2 if (kind == "gm" and half < 2) or (kind == "wm" and half == 0) else 1
                slots_at[kind, half, t] = range(s, min(s + n, N_UNITS + 3))
                s = min(s + n, N_UNITS + 3)
    assert s == N_UNITS + 3

    with ExitStack() as ctx:
        names = []

        def sb(name, shape, dt=F32, stack=ctx):
            return stack.enter_context(nc.sbuf_tensor(name, shape, dt))

        def sem(name):
            return ctx.enter_context(nc.semaphore(name))

        def shared(stack, *lives):
            made = []
            for n, life in enumerate(lives):
                with ExitStack() as own:
                    made.append([sb(name, shape, dt, own) for name, shape, dt in life])
                    if n == len(lives) - 1:
                        stack.push(own.pop_all())
            return made

        ident = sb("ident", [P, P])
        cst = sb("cst", [P, 3 * 2 * FT + 44])
        raw = [sb(f"raw{i}", [P, PANEL]) for i in range(2)]
        whi = [sb(f"whi{i}", [P, PANEL], F32R) for i in range(2)]
        wlo = [sb(f"wlo{i}", [P, PANEL], F32R) for i in range(2)]
        xn_hi = sb("xn_hi", [P, KD, T], F32R)
        xn_lo = sb("xn_lo", [P, KD, T], F32R)
        m_half = sb("m_half", [P, 8])
        stats = sb("stats", [P, 64])
        n_ss, n_ms, n_rs = (stats[:, 10 * i:10 * i + 10] for i in range(3))
        e_max, e_sum, e_inv = (stats[:, 32 + 4 * i:36 + 4 * i] for i in range(3))
        c_stats = sb("c_stats", [P, 2, 24])
        wi = sb("wi", [P, TB * IH])

        first = ExitStack()
        early = first
        (x_tok,), (ya_hi, ya_lo), (t_y,) = shared(
            early, [("x_tok", [P, TB, D], F32)],
            [("ya_hi", [P, 4, T], F32R), ("ya_lo", [P, 4, T], F32R)], [("t_y", [P, KD, T], F32)])
        (memn_hi, memn_lo), (ym_hi, ym_lo) = shared(
            early, [("memn_hi", [P, KD, M], F32R), ("memn_lo", [P, KD, M], F32R)],
            [("ym_hi", [P, 4, T], F32R), ("ym_lo", [P, 4, T], F32R)])
        (mem_tok,), (cbuf, cvbuf), (t_am,) = shared(
            early, [("mem_tok", [P, MB, D], F32)], [("cbuf", [P, 2, T], F32), ("cvbuf", [P, 2, T], F32)],
            [("t_am", [P, 4, T], F32)])
        (sq, qn, wiT, rl, nt), (merged,) = shared(
            early, [("sq", [P, T], F32), ("qn", [P, 2, T], F32), ("wiT", [IH, T], F32), ("rl", [P, 2, T], F32),
                    ("nt", [P, 2, T], F32)],
            [("merged", [P, KD, T], F32)])
        qT = sb("qT", [P, 4, T], F32, early)
        kT = sb("kT", [P, 4, T], F32, early)
        v = sb("v", [P, TB, AW], F32, early)
        (stage_a, stage_b), (qmT, kmT, vm), (yb_hi, yb_lo) = shared(
            early, [("stage_a", [2 * FT, 3, P], F32), ("stage_b", [40, P], F32)], [("qmT", [P, 4, T], F32), ("kmT", [P, 4, M], F32),
                                                                   ("vm", [P, MB, AW], F32)],
            [("yb_hi", [P, 4, T], F32R), ("yb_lo", [P, 4, T], F32R)])
        (qiT, kiT), (prob, probT) = shared(
            early, [("qiT", [P, 2, T], F32), ("kiT", [P, T], F32)],
            [("prob", [P, 3, T], F32), ("probT", [P, 2, T], F32)])
        offset = {1: 0, 2: 256, 3: 640}
        score = sb("score", [P, 1152], F32, early)
        work = sb("work", [P, 1152], F32, early)
        m8 = sb("m8", [P, 8], F32, early)
        far = [sb(f"far{b}", [P, (b + 1) * P], F32, early) for b in range(TB)]
        causal = sb("causal", [P, P], F32, early)
        first.close()
        second = ctx
        x2 = sb("x2", [P, TB, D], F32, second)
        xs2 = sb("xs2", [P, TB, D], F32, second)
        xn2_hi = sb("xn2_hi", [P, KD, T], F32R, second)
        xn2_lo = sb("xn2_lo", [P, KD, T], F32R, second)
        hraw = sb("hraw", [P, FT, T], F32, second)
        taps = sb("taps", [P, 4, T], F32, second)

        banks = [ctx.enter_context(nc.psum_tensor(f"bank{i}", [P, T], F32)) for i in range(8)]
        s_bank, t_bank, o_bank = banks[4:6], banks[6], banks[7]

        x_landed = [sem(f"x_landed{i}") for i in range(TB)]
        mem_landed, small_landed, x2_landed, stored = sem("mem_landed"), sem("small_landed"), sem("x2_landed"), sem("stored")
        raw_landed = [sem("raw_landed0"), sem("raw_landed1")]
        hi_done, lo_done, panel_used = sem("hi_done"), sem("lo_done"), sem("panel_used")
        bank_ready = sem("bank_ready")
        bank_read = {"act": sem("bank_read_act"), "dve": sem("bank_read_dve")}
        pool_const, cst_ready, cst_done = sem("pool_const"), sem("cst_ready"), sem("cst_done")
        n_sum, n_mean, n_rstd, n_scaled, n_hi, n_lo = (sem(f"norm_{s}") for s in ("sum", "mean", "rstd", "scaled", "hi", "lo"))
        c_sq, c_mean, c_rstd = sem("chain_sq"), sem("chain_mean"), sem("chain_rstd")
        t_ready, t_read = sem("turned"), sem("turned_read")
        s_ready = sem("score_ready")
        s_read = {"act": sem("score_read_act"), "dve": sem("score_read_dve")}
        ki_ready, qi_ready, wiT_ready, rl_used = sem("ki_ready"), sem("qi_ready"), sem("wiT_ready"), sem("rl_used")
        v_ready, vm_ready = sem("v_ready"), sem("vm_ready")
        max_done, exp_done, prob_done, o_ready, o_hi, o_lo = (sem(s) for s in ("max_done", "exp_done", "prob_done", "o_ready", "o_hi", "o_lo"))
        conv_done, ya_hi_done, ya_lo_done = sem("conv_done"), sem("ya_hi_done"), sem("ya_lo_done")
        t_used, merged_done, mg_hi, mg_lo = sem("gate_used"), sem("merged_done"), sem("mg_hi"), sem("mg_lo")
        tap_done, tap_step, silu_done, pair_done = sem("tap_done"), sem("tap_step"), sem("silu_done"), sem("pair_done")
        h_hi, h_lo, out_done = sem("h_hi"), sem("h_lo"), sem("out_done")
        dve_step = sem("dve_step")

        tap_f = lambda tap, tile: tap * 2 * FT + tile
        G0 = 3 * 2 * FT
        col = lambda i: cst[:, i:i + 1]
        g_cols = {"x": G0, "mem": G0 + 8, "x2": G0 + 16}
        tap_a = lambda tap, tile: G0 + 24 + tap * 4 + tile
        gain = {"k": G0 + 37, "km": G0 + 39, "q": G0 + 40, "qm": G0 + 41}

        def count(readers, who, upto):
            return readers[:upto + 1].count(who)

        def panel(slot, k):
            return [w[slot][:, :].rearrange("p (k n) -> p k n", k=k) for w in (whi, wlo)]

        def small_panel(slot, k, n):
            return [w[slot][:, 0:k * n].rearrange("p (k n) -> p k n", k=k) for w in (whi, wlo)]

        NORMS = [("x", b) for b in range(TB)] + [("mem", b) for b in range(MB)] + [("x2", b) for b in range(TB)]

        def norm_place(i):
            kind, b = NORMS[i]
            src = {"x": x_tok, "mem": mem_tok, "x2": x2}[kind][:, b, :]
            dst = {"x": x_tok, "mem": mem_tok, "x2": xs2}[kind][:, b, :]
            hi, lo = {"x": (xn_hi, xn_lo), "mem": (memn_hi, memn_lo), "x2": (xn2_hi, xn2_lo)}[kind]
            use = bank_uses[{"x": "xT", "mem": "memT", "x2": "x2T"}[kind], 0] + 2 * b
            tmp = [taps[:, h, :] if kind == "x2" else nt[:, h, :] for h in range(2)]
            return kind, b, src, dst, hi, lo, use, tmp

        CHAINS = [(kind, half, i) for kind in ("k", "q", "qm", "km") for half in range(2)
                  for i in range(1 if kind == "km" else 2)]
        assert len(CHAINS) == N_CHAINS
        chain_of = {c: n for n, c in enumerate(CHAINS)}

        def chain_shape(kind):
            g = HD if kind in "qk" else MHD
            return g, T // g

        chain_dst = {"k": kT, "q": qT, "qm": qmT, "km": kmT}
        gate_slot = lambda g: t_am[:, g % 4, :] if g < 16 else t_y[:, g - 16, :]

        block = ctx.enter_context(nc.Block())

        @block.sync
        def _(sp):
            for b in range(TB):
                sp.dma_start(x_tok[:, b, :], x[0, b * P:(b + 1) * P, :]).then_inc(x_landed[b], 16)

            def slot_free(p):
                sp.wait_ge(lo_done, 2 * (p - 1))

            for p, (_, _, src) in enumerate(panels):
                if p >= 2:
                    slot_free(p)
                k, n = src.shape[1:]
                dst = raw[p % 2][:, 0:k * n].rearrange("p (k n) -> p k n", k=k)
                sp.dma_start(dst, src).then_inc(raw_landed[p % 2], 16)
            with sp.Fori(0, FT // 2) as it:
                for s in range(2):
                    slot_free(it * 2 + (UP0 + s))
                    sp.dma_start(raw[s][:, :].rearrange("p (k n) -> p k n", k=KD),
                                 wup[:, :, bass.ds(it * COLS + s * FF, COLS)]).then_inc(raw_landed[s], 16)
            for d in range(N_DOWN):
                slot_free(DOWN0 + d)
                sp.dma_start(raw[d % 2][:, :].rearrange("p (k n) -> p k n", k=2),
                             wdown[:, 2 * d:2 * d + 2, :]).then_inc(raw_landed[d % 2], 16)
            for n in range(8):
                b, half = n // 2, n % 2
                sp.wait_ge(out_done, n + 1)
                sp.dma_start(out[0, b * P:(b + 1) * P, half * 512:half * 512 + 512],
                             x2[:, b, half * 512:half * 512 + 512]).then_inc(stored, 16)
            sp.wait_ge(stored, 8 * 16)

        @block.gpsimd
        def _(pool):
            pool.memset(ident[:, :], 0.0).then_inc(pool_const, 1)
            pool.wait_ge(pool_const, 1)
            pool.affine_select(out=ident[:, :], in_=ident[:, :], compare_op=ALU.not_equal, fill=1.0, base=0,
                               pattern=[[-1, P]], channel_multiplier=1).then_inc(pool_const, 1)
            pool.memset(m_half[:, :], -0.5).then_inc(pool_const, 1)
            pool.wait_ge(pool_const, 3)

            def norm_rstd(i):
                pool.wait_ge(n_mean, i + 1)
                pool.tensor_tensor(n_rs[:, i:i + 1], n_ms[:, i:i + 1], m_half[:, 0:1], ALU.pow).then_inc(n_rstd, 1)

            for i in range(TB):
                norm_rstd(i)
            for b in range(TB):
                pool.iota(far[b][:, :], pattern=[[-1, (b + 1) * P]], base=b * P, channel_multiplier=1,
                          allow_small_or_imprecise_dtypes=True).then_inc(pool_const, 1)
            pool.memset(causal[:, :], 0.0).then_inc(pool_const, 1)
            pool.wait_ge(pool_const, 4 + TB)
            pool.affine_select(out=far[0][:, :], in_=far[0][:, :], compare_op=ALU.is_ge, fill=FAR, base=0,
                               pattern=[[-1, P]], channel_multiplier=1).then_inc(pool_const, 1)
            pool.affine_select(out=causal[:, :], in_=causal[:, :], compare_op=ALU.is_ge, fill=-1e38, base=0,
                               pattern=[[-1, P]], channel_multiplier=1).then_inc(pool_const, 1)

            def chain_rstd(c):
                _, n = chain_shape(CHAINS[c][0])
                pool.wait_ge(c_mean, c + 1)
                pool.tensor_tensor(c_stats[:, c % 2, 16:16 + n], c_stats[:, c % 2, 8:8 + n], m_half[:, 0:n],
                                   ALU.pow).then_inc(c_rstd, 1)

            for c in range(8):
                chain_rstd(c)
            for i in range(TB, TB + MB):
                norm_rstd(i)
            for c in range(8, N_CHAINS):
                chain_rstd(c)
            pool.wait_ge(merged_done, KD)
            for b in range(TB):
                pool.dma_start(x2[:, b, :], x[0, b * P:(b + 1) * P, :]).then_inc(x2_landed, 16)
            for i in range(TB + MB, len(NORMS)):
                norm_rstd(i)

        @block.scalar
        def _(act):
            act.dma_start(stage_b[0:8, :], g_mix[0].rearrange("(k p) -> k p", p=P)).then_inc(small_landed, 16)
            act.dma_start(stage_b[8:16, :], g_mem[0].rearrange("(k p) -> k p", p=P)).then_inc(small_landed, 16)
            act.dma_start(stage_b[16:24, :], g_ffn[0].rearrange("(k p) -> k p", p=P)).then_inc(small_landed, 16)
            for tap in range(3):
                act.dma_start(stage_b[24 + 4 * tap:28 + 4 * tap, :],
                              conv_a_w[0, tap].rearrange("(k p) -> k p", p=P)).then_inc(small_landed, 16)
            for r, g in enumerate((q_norm_g, k_norm_g)):
                for h in range(2):
                    act.dma_start(stage_b[36 + r:37 + r, h * HD:(h + 1) * HD], g).then_inc(small_landed, 16)
            for r, g in enumerate((mq_norm_g, mk_norm_g)):
                act.dma_start(stage_b[38 + r:39 + r, :], g).then_inc(small_landed, 16)
            act.dma_start(stage_a[:, :, :], conv_f_w[0].rearrange("t (j p) -> j t p", p=P)).then_inc(small_landed, 16)
            act.dma_start(mem_tok[:, :, :], mem[0].rearrange("(b p) d -> p b d", p=P)).then_inc(mem_landed, 16)

            def split_hi(p, n, slot):
                for piece in range(2):
                    sl = slice(piece * n // 2, (piece + 1) * n // 2)
                    act.activation(whi[slot][:, sl], raw[slot][:, sl], ACT.Copy).then_inc(hi_done, 1)

            def split_head(p):
                if p >= 2:
                    act.wait_ge(panel_used, p - 1)
                act.wait_ge(raw_landed[p % 2], 16 * (p // 2 + 1))
                n = panels[p][2].shape[1] * panels[p][2].shape[2] if p < N_HEAD else PANEL
                split_hi(p, n, p % 2)

            def norm_sum(i):
                kind, b, src, dst, *_ = norm_place(i)
                if kind == "x":
                    act.wait_ge(x_landed[b], 16)
                elif kind == "mem":
                    act.wait_ge(mem_landed, 16)
                else:
                    act.wait_ge(bank_read["dve"], count(last_reader, "dve", bank_uses["wo", 2] + b))
                if i >= 1:
                    act.wait_ge(n_sum, i)
                scratch = {"x": score[:, 0:D], "mem": qmT[:, 0:2, :].rearrange("p a t -> p (a t)"), "x2": xs2[:, b, :]}[kind]
                act.activation(scratch, src, ACT.Square, accum_out=n_ss[:, i:i + 1]).then_inc(n_sum, 1)

            def norm_hi(i, half):
                kind, b, src, dst, hi, lo, use, tmp = norm_place(i)
                act.wait_ge(bank_read["dve"], count(last_reader, "dve", use + half))
                act.activation(hi[:, 4 * half:4 * half + 4, b * P:(b + 1) * P],
                               tmp[half].rearrange("p (k t) -> p k t", k=4), ACT.Copy).then_inc(n_hi, 1)

            def chain_square(c, use):
                act.wait_ge(bank_ready, use + 1)
                if c >= 1:
                    act.wait_ge(c_mean, c)
                act.activation(sq[:, :], banks[use % 4][:, :], ACT.Square).then_inc(c_sq, 1)

            def chain_gain(c):
                kind, half, i = CHAINS[c]
                act.wait_ge(t_ready, c + 2)
                act.wait_ge(cst_done, 1)
                dst = chain_dst[kind][:, 2 * half:2 * half + 2, 2 * i * P:2 * i * P + 2 * P]
                act.activation(dst, t_bank[:, :].rearrange("p (c t) -> p c t", c=2), ACT.Copy,
                               scale=col(gain[kind])).then_inc(t_read, 1)

            def idx_relu(u):
                act.wait_ge(s_ready, u + 1)
                if u >= 2:
                    act.wait_ge(rl_used, u - 1)
                b, _ = IDX[u]
                n = (b + 1) * P
                act.activation(rl[:, u % 2, 0:n], s_bank[u % 2][:, 0:n], ACT.Relu).then_inc(s_read["act"], 1)

            def slot(s):
                if 0 <= s - 2 < N_UNITS:
                    u = s - 2
                    kind, h, b = UNITS[u]
                    act.wait_ge(t_ready, PT0 + u + 1)
                    if u >= 2:
                        act.wait_ge(o_ready, u - 1)
                    n = keys(kind, b)
                    act.activation(probT[:, u % 2, 0:n], t_bank[:, 0:n], ACT.Copy).then_inc(t_read, 1)
                if s - 3 in group_end:
                    g = group_end[s - 3]
                    act.wait_ge(o_ready, s - 2)
                    dst = ym_hi[:, g, :] if g < 4 else yb_hi[:, g - 4, :]
                    act.activation(dst, o_bank[:, :], ACT.Copy).then_inc(o_hi, 1)
                if s < N_UNITS:
                    kind, h, b = UNITS[s]
                    n = keys(kind, b)
                    act.wait_ge(max_done, s + 1)
                    if kind == "m" and s >= 3:
                        act.wait_ge(t_ready, PT0 + s - 2)
                    src = s_bank[(len(IDX) + s) % 2][:, 0:n] if kind == "m" else prob[:, s % 3, 0:n]
                    ins = act.activation(prob[:, s % 3, 0:n], src, ACT.Exp, bias=e_max[:, s % 4:s % 4 + 1],
                                         accum_out=e_sum[:, s % 4:s % 4 + 1])
                    ins.then_inc(exp_done, 1)

            split_head(0)
            for i in range(TB):
                norm_sum(i)
            split_head(1)
            for i in range(TB):
                for half in range(2):
                    norm_hi(i, half)

            pending = None
            idx = 0
            for p, (kind, half, src) in enumerate(panels):
                if kind == "qm" and half == 0:
                    for i in range(TB, TB + MB):
                        norm_sum(i)
                    for i in range(TB, TB + MB):
                        for h in range(2):
                            norm_hi(i, h)
                if kind == "wo":
                    use, n_banks = 0, 0
                else:
                    use = bank_uses[kind, half]
                    n_banks = per_panel[kind if kind in per_panel else kind[0]][0]
                for t in range(n_banks):
                    n = use + t
                    ps = banks[n % 4]
                    if kind in ("k", "q", "qm", "km"):
                        chain_square(chain_of[kind, half, t], n)
                    elif kind == "ki":
                        act.wait_ge(bank_ready, n + 1)
                        act.activation(wiT[:, :], ps[ID:ID + IH, :], ACT.Copy).then_inc(wiT_ready, 1)
                        for r in range(3):
                            act.activation(kiT[r * ID:(r + 1) * ID, :], ps[0:ID, :], ACT.Copy).then_inc(ki_ready, 1)
                        act.activation(kiT[3 * ID:4 * ID, :], ps[0:ID, :], ACT.Copy).then_inc(bank_read["act"], 1)
                    elif kind == "qi":
                        act.wait_ge(bank_ready, n + 1)
                        act.activation(qiT[:, t, :], ps[:, :], ACT.Copy).then_inc(bank_read["act"], 1)
                        if t == 1:
                            act.wait_ge(t_ready, 1)
                            act.activation(wi[:, :], t_bank[:, 0:TB * IH], ACT.Copy).then_inc(t_read, 1)
                    elif kind in ("v", "vm"):
                        act.wait_ge(bank_ready, n + 1)
                        dst = (v if kind == "v" else vm)[:, 2 * t:2 * t + 2, half * COLS:(half + 1) * COLS]
                        act.activation(dst, ps[:, :].rearrange("p (b n) -> p b n", b=2), ACT.Copy)\
                           .then_inc(bank_read["act"], 1)
                    elif kind == "c":
                        act.wait_ge(bank_ready, n + 1)
                        if half == 1:
                            act.wait_ge(conv_done, t + 1)
                        act.activation(cbuf[:, t, :], ps[:, :], ACT.Copy).then_inc(bank_read["act"], 1)
                    elif kind == "b":
                        act.wait_ge(bank_read["dve"], count(last_reader, "dve", n))
                        act.activation(ya_hi[:, 2 * half + t, :], cvbuf[:, t, :], ACT.Copy).then_inc(ya_hi_done, 1)
                    elif kind[0] == "g":
                        g = {"a": 0, "m": 8, "y": 16}[kind[1]] + 2 * half + t
                        act.wait_ge(bank_ready, n + 1)
                        if 4 <= g < 16:
                            act.wait_ge(t_used, g - 3)
                        act.activation(gate_slot(g), ps[:, :], ACT.Tanh, scale=0.5).then_inc(bank_read["act"], 1)
                    elif kind == "wy":
                        j = 4 * half + t
                        act.wait_ge(merged_done, j + 1)
                        act.activation(xn_hi[:, j, :], merged[:, j, :], ACT.Copy, scale=0.5).then_inc(mg_hi, 1)
                    if pending is not None:
                        chain_gain(pending)
                        pending = None
                    if kind in ("k", "q", "qm", "km"):
                        pending = chain_of[kind, half, t]
                    if kind in ("k", "q"):
                        for _ in range(3):
                            idx_relu(idx)
                            idx += 1
                    for s in slots_at.get((kind, half, t), ()):
                        slot(s)
                if p + 2 < N_HEAD + 2:
                    split_head(p + 2)
            for i in range(TB + MB, len(NORMS)):
                norm_sum(i)
            for i in range(TB + MB, len(NORMS)):
                for half in range(2):
                    norm_hi(i, half)

            with act.Fori(0, FT // 2) as it:
                for q in range(4):
                    i = q % 2
                    act.wait_ge(bank_ready, it * 4 + (N_USES + q + 1))
                    act.wait_ge(pair_done, it * 2 + (i + 1))
                    act.activation(taps[:, q, :], banks[(N_USES + q) % 4][:, :], ACT.Copy,
                                   scale=cst[:, bass.ds(it * 2 + tap_f(2, (q // 2) * FT + i), 1)]).then_inc(tap_done, 1)
                    if i == 1:
                        p = it * 2 + (UP0 + q // 2 + 2)
                        act.wait_ge(panel_used, p - 1)
                        act.wait_ge(raw_landed[q // 2], it * 16 + 16 * ((UP0 + q // 2 + 2) // 2 + 1))
                        split_hi(p, PANEL, q // 2)
                    if q == 1:
                        for g in range(2):
                            act.wait_ge(bank_read["dve"], it * 4 + (DVE_USES + g + 1))
                            act.activation(taps[:, g, :], taps[:, g, :], ACT.Silu).then_inc(silu_done, 1)

            def split_h_hi(d, slot):
                for c in range(2):
                    act.activation(xn2_hi[:, 2 * slot + c, :], hraw[:, bass.ds(d * 2 + c, 1), :].squeeze(1),
                                   ACT.Copy).then_inc(h_hi, 1)

            act.wait_ge(bank_ready, N_USES + 2 * FT)
            act.wait_ge(pair_done, FT + 2)
            for d in range(2):
                split_h_hi(d, d)

            def down_next(d, slot):
                act.wait_ge(panel_used, d + (DOWN0 + 1))
                act.wait_ge(raw_landed[slot], (d - slot) * 8 + 16 * (DOWN0 // 2 + 2))
                split_hi(None, PANEL, slot)
                split_h_hi(d + 2, slot)

            down_next(0, 0)
            with act.Fori(0, (N_DOWN - 3) // 2) as it:
                down_next(it * 2 + 1, 1)
                down_next(it * 2 + 2, 0)

        @block.vector
        def _(dve):
            steps = [0]

            def link(ins):
                steps[0] += 1
                ins.then_inc(dve_step, 1)
                dve.wait_ge(dve_step, steps[0])

            def split_lo(slot, n, hi_value):
                for piece in range(2):
                    sl = slice(piece * n // 2, (piece + 1) * n // 2)
                    dve.wait_ge(hi_done, hi_value + (piece + 1))
                    dve.tensor_tensor(wlo[slot][:, sl], raw[slot][:, sl], whi[slot][:, sl], ALU.subtract)\
                       .then_inc(lo_done, 1)

            def split_head(p):
                n = panels[p][2].shape[1] * panels[p][2].shape[2] if p < N_HEAD else PANEL
                split_lo(p % 2, n, 2 * p)

            def norm_mean(i):
                dve.wait_ge(n_sum, i + 1)
                dve.tensor_scalar(n_ms[:, i:i + 1], n_ss[:, i:i + 1], 1.0 / D, EPS, ALU.mult, ALU.add)\
                   .then_inc(n_mean, 1)

            def norm_scale(i):
                _, _, src, dst, *_ = norm_place(i)
                dve.wait_ge(n_rstd, i + 1)
                dve.tensor_scalar(dst, src, n_rs[:, i:i + 1], None, ALU.mult).then_inc(n_scaled, 1)

            def norm_gain(i, half):
                kind, b, _, _, hi, lo, use, tmp = norm_place(i)
                dve.wait_ge(bank_ready, use + half + 1)
                if 2 * i + half >= 2:
                    dve.wait_ge(n_lo, 2 * i + half - 1)
                g0 = g_cols[kind] + 4 * half
                g = cst[:, g0:g0 + 4].unsqueeze(2).to_broadcast([P, 4, P])
                dve.tensor_tensor(tmp[half].rearrange("p (k t) -> p k t", k=4),
                                  banks[(use + half) % 4][:, :].rearrange("p (k t) -> p k t", k=4), g,
                                  ALU.mult).then_inc(bank_read["dve"], 1)

            def norm_lo(i, half):
                _, b, _, _, hi, lo, use, tmp = norm_place(i)
                dve.wait_ge(n_hi, 2 * i + half + 1)
                at = (slice(None), slice(4 * half, 4 * half + 4), slice(b * P, (b + 1) * P))
                dve.tensor_tensor(lo[at], tmp[half].rearrange("p (k t) -> p k t", k=4), hi[at],
                                  ALU.subtract).then_inc(n_lo, 1)

            def norm_turned(blocks):
                last = None
                for i in blocks:
                    for half in range(2):
                        norm_gain(i, half)
                        if last is not None:
                            norm_lo(*last)
                        last = (i, half)
                norm_lo(*last)

            def chain_stat(c):
                g, n = chain_shape(CHAINS[c][0])
                st = c_stats[:, c % 2, :]
                dve.wait_ge(c_sq, c + 1)
                link(dve.tensor_reduce(st[:, 0:n], sq[:, :].rearrange("p (n g) -> p n g", g=g), AX.X, ALU.add))
                dve.tensor_scalar(st[:, 8:8 + n], st[:, 0:n], 1.0 / g, EPS, ALU.mult, ALU.add).then_inc(c_mean, 1)

            def chain_norm(c, use):
                g, n = chain_shape(CHAINS[c][0])
                dve.wait_ge(c_rstd, c + 1)
                if c >= 2:
                    dve.wait_ge(t_ready, c)
                r = c_stats[:, c % 2, 16:16 + n].unsqueeze(2).to_broadcast([P, n, g])
                dve.tensor_tensor(qn[:, c % 2, :].rearrange("p (n g) -> p n g", g=g),
                                  banks[use % 4][:, :].rearrange("p (n g) -> p n g", g=g), r,
                                  ALU.mult).then_inc(bank_read["dve"], 1)

            def idx_add(u):
                b, h = IDX[u]
                n = (b + 1) * P
                sc = score[:, offset[b]:offset[b] + n]
                w = wi[:, b * IH + h:b * IH + h + 1]
                dve.wait_ge(s_read["act"], u + 1)
                if u == 0:
                    dve.wait_ge(t_read, 1)
                if h == 0:
                    dve.tensor_scalar(sc, rl[:, u % 2, 0:n], w, 0.0, ALU.mult, ALU.add).then_inc(rl_used, 1)
                else:
                    dve.wait_ge(rl_used, u)
                    dve.scalar_tensor_tensor(sc, rl[:, u % 2, 0:n], w, sc, ALU.mult, ALU.add).then_inc(rl_used, 1)
                if h == IH - 1:
                    dve.wait_ge(rl_used, u + 1)
                    dve.wait_ge(pool_const, 6 + TB)
                    diag = score[:, offset[b] + b * P:offset[b] + n]
                    link(dve.tensor_tensor(diag, diag, causal[:, :], ALU.add))

            def topk_round(r):
                b, r = 1 + r // (TOPK // 8), r % (TOPK // 8)
                n = (b + 1) * P
                sc, wk = score[:, offset[b]:offset[b] + n], work[:, offset[b]:offset[b] + n]
                src = sc if r == 0 else wk
                link(dve.max(m8[:, :], src))
                link(dve.match_replace(wk, m8[:, :], src, FILL))
                if r == TOPK // 8 - 1:
                    link(dve.scalar_tensor_tensor(wk, wk, 1.0, sc, ALU.mult, ALU.is_equal))
                    link(dve.scalar_tensor_tensor(far[b][:, :], wk, FAR, far[b][:, :], ALU.mult, ALU.add))

            def slot(s):
                if 0 <= s - 1 < N_UNITS:
                    u = s - 1
                    kind, h, b = UNITS[u]
                    pr = prob[:, u % 3, 0:keys(kind, b)]
                    dve.wait_ge(exp_done, u + 1)
                    link(dve.reciprocal(e_inv[:, u % 4:u % 4 + 1], e_sum[:, u % 4:u % 4 + 1]))
                    dve.tensor_scalar(pr, pr, e_inv[:, u % 4:u % 4 + 1], None, ALU.mult).then_inc(prob_done, 1)
                if s < N_UNITS:
                    kind, h, b = UNITS[s]
                    n = keys(kind, b)
                    dve.wait_ge(s_ready, len(IDX) + s + 1)
                    ps = s_bank[(len(IDX) + s) % 2][:, 0:n]
                    if kind == "s":
                        slope = 2.0 ** -(h + 1)
                        dve.wait_ge(t_ready, PT0 + s - 2)
                        dve.scalar_tensor_tensor(prob[:, s % 3, 0:n], far[b][:, :], -slope, ps, ALU.mult, ALU.add)\
                           .then_inc(s_read["dve"], 1)
                        dve.wait_ge(s_read["dve"], count(score_reader, "dve", len(IDX) + s))
                        ps = prob[:, s % 3, 0:n]
                    dve.tensor_reduce(e_max[:, s % 4:s % 4 + 1], ps, AX.X, ALU.max, negate=True).then_inc(max_done, 1)
                if s - 3 in group_end:
                    g = group_end[s - 3]
                    hi, lo = (ym_hi, ym_lo) if g < 4 else (yb_hi, yb_lo)
                    dve.wait_ge(o_hi, g + 1)
                    dve.tensor_tensor(lo[:, g % 4, :], o_bank[:, :], hi[:, g % 4, :], ALU.subtract).then_inc(o_lo, 1)

            dve.wait_ge(cst_ready, 1)
            link(dve.tensor_copy(cst[:, 0:G0 + 40], o_bank[:, 0:G0 + 40]))
            link(dve.tensor_scalar(cst[:, G0 + 40:G0 + 41], cst[:, G0 + 36:G0 + 37], HD ** -0.5, None, ALU.mult))
            dve.tensor_scalar(cst[:, G0 + 41:G0 + 42], cst[:, G0 + 38:G0 + 39], MHD ** -0.5, None, ALU.mult)\
               .then_inc(cst_done, 1)
            split_head(0)
            for i in range(TB):
                norm_mean(i)
                norm_scale(i)
            split_head(1)
            norm_turned(range(TB))

            idx, rounds = 0, 0
            for p, (kind, half, src) in enumerate(panels):
                if kind == "qm" and half == 0:
                    for i in range(TB, TB + MB):
                        norm_mean(i)
                        norm_scale(i)
                    norm_turned(range(TB, TB + MB))
                if kind == "wo":
                    use, n_banks = bank_uses[kind, half - half % 2], 4 * (half % 2)
                else:
                    use = bank_uses[kind, half]
                    n_banks = per_panel[kind if kind in per_panel else kind[0]][0]
                for t in range(n_banks):
                    n = use + t
                    ps = banks[n % 4][:, :]
                    if kind in ("k", "q", "qm", "km"):
                        chain_stat(chain_of[kind, half, t])
                    if kind in ("k", "q"):
                        for _ in range(3):
                            idx_add(idx)
                            idx += 1
                    if kind in ("v", "qm", "km", "vm", "c", "h", "b"):
                        for _ in range(2):
                            topk_round(rounds)
                            rounds += 1
                    if kind in ("k", "q", "qm", "km"):
                        chain_norm(chain_of[kind, half, t], n)
                    elif kind == "h":
                        j = 2 * half + t
                        u, cv = cbuf[:, t, :], cvbuf[:, t, :]
                        dve.wait_ge(bank_ready, n + 1)
                        dve.wait_ge(bank_read["act"], count(last_reader, "act", bank_uses["c", half] + t))
                        if half == 1:
                            dve.wait_ge(ya_lo_done, t + 1)
                        dve.tensor_tensor(u, u, ps, ALU.mult).then_inc(bank_read["dve"], 1)
                        dve.wait_ge(bank_read["dve"], count(last_reader, "dve", n))
                        link(dve.tensor_scalar(cv, u, col(tap_a(2, j)), None, ALU.mult))
                        link(dve.scalar_tensor_tensor(cv[:, 1:T], u[:, 0:T - 1], col(tap_a(1, j)), cv[:, 1:T],
                                                      ALU.mult, ALU.add))
                        dve.scalar_tensor_tensor(cv[:, 2:T], u[:, 0:T - 2], col(tap_a(0, j)), cv[:, 2:T],
                                                 ALU.mult, ALU.add).then_inc(conv_done, 1)
                    elif kind == "b":
                        j = 2 * half + t
                        cv = cvbuf[:, t, :]
                        dve.wait_ge(bank_ready, n + 1)
                        dve.wait_ge(conv_done, j + 1)
                        dve.tensor_tensor(cv, cv, ps, ALU.mult).then_inc(bank_read["dve"], 1)
                        dve.wait_ge(ya_hi_done, j + 1)
                        dve.tensor_tensor(ya_lo[:, j, :], cv, ya_hi[:, j, :], ALU.subtract).then_inc(ya_lo_done, 1)
                    elif kind[0] == "w" and kind != "wo":
                        g = {"a": 0, "m": 8, "y": 16}[kind[1]] + 4 * half + t
                        j = 4 * half + t
                        gt = gate_slot(g)
                        dve.wait_ge(bank_ready, n + 1)
                        dve.wait_ge(bank_read["act"], count(last_reader, "act",
                                                            bank_uses["g" + kind[1], 2 * half + t // 2] + t % 2))
                        mg = merged[:, j, :]
                        if kind == "wa":
                            dve.scalar_tensor_tensor(mg, gt, 1.0, ps, ALU.add, ALU.mult).then_inc(bank_read["dve"], 1)
                            dve.wait_ge(bank_read["dve"], count(last_reader, "dve", n))
                            dve.sem_inc(t_used, 1)
                        else:
                            dve.scalar_tensor_tensor(gt, gt, 1.0, ps, ALU.add, ALU.mult).then_inc(bank_read["dve"], 1)
                            dve.wait_ge(bank_read["dve"], count(last_reader, "dve", n))
                            done = t_used if kind == "wm" else merged_done
                            dve.tensor_tensor(mg, mg, gt, ALU.add).then_inc(done, 1)
                        if kind == "wy":
                            dve.wait_ge(mg_hi, j + 1)
                            dve.scalar_tensor_tensor(xn_lo[:, j, :], mg, 0.5, xn_hi[:, j, :], ALU.mult,
                                                     ALU.subtract).then_inc(mg_lo, 1)
                    elif kind == "wo":
                        at = x2[:, t, (half // 2) * 512:(half // 2) * 512 + 512]
                        dve.wait_ge(bank_ready, n + 1)
                        dve.wait_ge(x2_landed, 16 * TB)
                        dve.tensor_tensor(at, at, ps, ALU.add).then_inc(bank_read["dve"], 1)
                    for s in slots_at.get((kind, half, t), ()):
                        slot(s)
                split_head(p + 2)
            assert rounds == 3 * TOPK // 8
            for i in range(TB + MB, len(NORMS)):
                norm_mean(i)
                norm_scale(i)
            norm_turned(range(TB + MB, len(NORMS)))
            dve.wait_ge(n_lo, 2 * len(NORMS))
            dve.sem_inc(pair_done, 2)

            with dve.Fori(0, FT // 2) as it:
                def hidden(i):
                    dve.wait_ge(silu_done, it * 2 + (i + 1))
                    dve.wait_ge(bank_read["dve"], it * 4 + (DVE_USES + 3 + i))
                    dve.tensor_tensor(hraw[:, bass.ds(it * 2 + i, 1), :].squeeze(1), taps[:, i, :],
                                      taps[:, 2 + i, :], ALU.mult).then_inc(pair_done, 1)

                for q in range(4):
                    i = q % 2
                    tile = (q // 2) * FT + i
                    ps = banks[(N_USES + q) % 4]
                    dve.wait_ge(tap_done, it * 4 + (q + 1))
                    dve.scalar_tensor_tensor(taps[:, q, 1:T], ps[:, 0:T - 1], cst[:, bass.ds(it * 2 + tap_f(1, tile), 1)],
                                             taps[:, q, 1:T], ALU.mult, ALU.add).then_inc(tap_step, 1)
                    dve.wait_ge(tap_step, it * 4 + (q + 1))
                    dve.scalar_tensor_tensor(taps[:, q, 2:T], ps[:, 0:T - 2], cst[:, bass.ds(it * 2 + tap_f(0, tile), 1)],
                                             taps[:, q, 2:T], ALU.mult, ALU.add).then_inc(bank_read["dve"], 1)
                    if i == 1:
                        split_lo(q // 2, PANEL, it * 4 + 2 * (UP0 + q // 2 + 2))
                for i in range(2):
                    hidden(i)

            def split_h_lo(d, slot):
                for c in range(2):
                    dve.wait_ge(h_hi, d * 2 + (c + 1))
                    dve.tensor_tensor(xn2_lo[:, 2 * slot + c, :], hraw[:, bass.ds(d * 2 + c, 1), :].squeeze(1),
                                      xn2_hi[:, 2 * slot + c, :], ALU.subtract).then_inc(h_lo, 1)

            for d in range(2):
                split_h_lo(d, d)

            def down_next(d, slot):
                split_lo(slot, PANEL, d * 2 + 2 * (DOWN0 + 2))
                split_h_lo(d + 2, slot)

            down_next(0, 0)
            with dve.Fori(0, (N_DOWN - 3) // 2) as it:
                down_next(it * 2 + 1, 1)
                down_next(it * 2 + 2, 0)
            for n in range(8):
                b, half = n // 2, n % 2
                at = x2[:, b, half * 512:half * 512 + 512]
                dve.wait_ge(bank_ready, N_USES + 2 * FT + n + 1)
                dve.tensor_tensor(at, at, banks[n][:, :], ALU.add).then_inc(out_done, 1)

        @block.tensor
        def _(pe):
            def product(o, a, b, start, stop):
                pe.matmul(o, a[0], b[0], start=start, stop=False)
                pe.matmul(o, a[0], b[1], start=False, stop=False)
                return pe.matmul(o, a[1], b[0], start=False, stop=stop)

            def bank_free(n):
                if n >= 4:
                    who = last_reader[n - 4]
                    pe.wait_ge(bank_read[who], count(last_reader, who, n - 4))

            def panel_there(p):
                pe.wait_ge(hi_done, p * 2 + 2)
                pe.wait_ge(lo_done, p * 2 + 2)

            def turn_norm(i):
                kind, b, _, dst, _, _, use, _ = norm_place(i)
                pe.wait_ge(n_scaled, i + 1)
                for half in range(2):
                    bank_free(use + half)
                    for k in range(4):
                        c = (4 * half + k) * P
                        last = pe.transpose(banks[(use + half) % 4][:, k * P:(k + 1) * P], dst[:, c:c + P], ident[:, :])
                    last.then_inc(bank_ready, 1)

            def turn_chain(c):
                kind, half, i = CHAINS[c]
                n = bank_uses[kind, half] + i
                pe.wait_ge(bank_read["dve"], count(last_reader, "dve", n))
                pe.wait_ge(t_read, c + 1)
                for cc in range(2):
                    for bb in range(2):
                        last = pe.transpose(t_bank[:, (2 * cc + bb) * P:(2 * cc + bb + 1) * P],
                                            qn[:, c % 2, bb * COLS + cc * P:bb * COLS + (cc + 1) * P], ident[:, :])
                last.then_inc(t_ready, 1)

            def score_bank(k):
                if k >= 2:
                    who = score_reader[k - 2]
                    if who == "exp":
                        pe.wait_ge(exp_done, k - 1 - len(IDX))
                    else:
                        pe.wait_ge(s_read[who], count(score_reader, who, k - 2))
                return s_bank[k % 2]

            def idx_scores(u):
                b, h = IDX[u]
                r = (h % 4) * ID
                ps = score_bank(u)
                if u == 0:
                    pe.wait_ge(bank_read["act"], count(last_reader, "act", bank_uses["qi", 0] + 1))
                    pe.wait_ge(ki_ready, 3)
                pe.matmul(ps[:, 0:(b + 1) * P], qiT[r:r + ID, h // 4, b * P:(b + 1) * P], kiT[r:r + ID, 0:(b + 1) * P],
                          start=True, stop=True).then_inc(s_ready, 1)

            def slot(s):
                if s < N_UNITS:
                    kind, h, b = UNITS[s]
                    n = keys(kind, b)
                    ps = score_bank(len(IDX) + s)
                    if kind == "m":
                        lhs, rhs = qmT[:, h, b * P:(b + 1) * P], kmT[:, h, :]
                    else:
                        r = (h % 2) * HD
                        lhs, rhs = qT[r:r + HD, h // 2, b * P:(b + 1) * P], kT[r:r + HD, h // 2, 0:n]
                    if s == 0:
                        pe.wait_ge(t_read, PT0)
                    pe.matmul(ps[:, 0:n], lhs, rhs, start=True, stop=True).then_inc(s_ready, 1)
                if 0 <= s - 2 < N_UNITS:
                    u = s - 2
                    kind, h, b = UNITS[u]
                    pe.wait_ge(prob_done, u + 1)
                    pe.wait_ge(t_read, PT0 + u)
                    for j in range(keys(kind, b) // P):
                        last = pe.transpose(t_bank[:, j * P:(j + 1) * P], prob[:, u % 3, j * P:(j + 1) * P], ident[:, :])
                    last.then_inc(t_ready, 1)
                if 0 <= s - 3 < N_UNITS:
                    u = s - 3
                    kind, h, b = UNITS[u]
                    n = keys(kind, b) // P
                    pe.wait_ge(t_read, PT0 + u + 1)
                    if u in group_start and group_start[u] > 0:
                        pe.wait_ge(o_lo, group_start[u])
                    if u == 0:
                        pe.wait_ge(bank_read["act"], count(last_reader, "act", bank_uses["vm", 1]))
                    for j in range(n):
                        if kind == "m":
                            o, lhs = o_bank[:, b * P:(b + 1) * P], vm[:, j, h * MHD:(h + 1) * MHD]
                        else:
                            r = (h % 2) * HD
                            o, lhs = o_bank[r:r + HD, b * P:(b + 1) * P], v[:, j, h * HD:(h + 1) * HD]
                        last = pe.matmul(o, lhs, probT[:, u % 2, j * P:(j + 1) * P], start=(j == 0), stop=(j == n - 1))
                    last.then_inc(o_ready, 1)

            pe.wait_ge(pool_const, 2)
            pe.wait_ge(small_landed, 16 * 13)
            for tap in range(3):
                pe.transpose(o_bank[:, tap_f(tap, 0):tap_f(tap, 2 * FT)], stage_a[:, tap, :],
                             ident[0:2 * FT, 0:2 * FT])
            pe.transpose(o_bank[:, G0:G0 + 40], stage_b[:, :], ident[0:40, 0:40]).then_inc(cst_ready, 1)
            for i in range(TB):
                turn_norm(i)
            pe.wait_ge(n_lo, 2 * TB)

            pending = None
            idx = 0
            for p, (kind, half, src) in enumerate(panels):
                k_in, cols = src.shape[1:]
                if kind == "qm" and half == 0:
                    for i in range(TB, TB + MB):
                        turn_norm(i)
                if kind == "km" and half == 0:
                    pe.wait_ge(n_lo, 2 * (TB + MB))
                panel_there(p)
                w = small_panel(p % 2, k_in, cols)
                xn = (xn_hi, xn_lo)
                if kind == "wo":
                    use, n_banks = bank_uses[kind, half - half % 2], 4
                else:
                    use = bank_uses[kind, half]
                    n_banks = per_panel[kind if kind in per_panel else kind[0]][0]
                for t in range(n_banks):
                    n = use + t
                    ps = banks[n % 4]
                    if kind != "wo" or half % 2 == 0:
                        bank_free(n)
                    if kind in ("k", "q", "v", "qm", "km", "vm"):
                        src_x = (memn_hi, memn_lo) if kind in ("km", "vm") else xn
                        for bb in range(2):
                            tok = slice((2 * t + bb) * P, (2 * t + bb + 1) * P)
                            for k in range(KD):
                                last = product(ps[:, bb * COLS:(bb + 1) * COLS], [a[:, k, tok] for a in src_x],
                                               [a[:, k, :] for a in w], k == 0, k == KD - 1)
                    elif kind == "wo":
                        kh = half % 2
                        if half == 0 and t == 0:
                            pe.wait_ge(mg_lo, KD)
                        for k in range(4):
                            last = product(ps[:, :], [a[:, 4 * kh + k, t * P:(t + 1) * P] for a in xn],
                                           [a[:, k, :] for a in w], kh == 0 and k == 0, kh == 1 and k == 3)
                    elif kind[0] == "w":
                        y, there = {"wa": ((ya_hi, ya_lo), (ya_lo_done, 4)), "wm": ((ym_hi, ym_lo), (o_lo, 4)),
                                    "wy": ((yb_hi, yb_lo), (o_lo, 8))}[kind]
                        pe.wait_ge(*there)
                        for k in range(4):
                            last = product(ps[:, :], [a[:, k, t * P:(t + 1) * P] for a in w],
                                           [a[:, k, :] for a in y], k == 0, k == 3)
                    else:
                        m = min(P, cols - t * P)
                        for k in range(KD):
                            last = product(ps[0:m, :], [a[:, k, t * P:t * P + m] for a in w],
                                           [a[:, k, :] for a in xn], k == 0, k == KD - 1)
                    if kind == "wo" and half % 2 == 0:
                        if t == n_banks - 1:
                            last.then_inc(panel_used, 1)
                    else:
                        last.then_inc(bank_ready, 1)
                    if t == n_banks - 1 and not (kind == "wo" and half % 2 == 0):
                        pe.wait_ge(bank_ready, n + 1)
                        pe.sem_inc(panel_used, 1)
                    if pending is not None:
                        turn_chain(pending)
                        pending = None
                    if kind in ("k", "q", "qm", "km"):
                        pending = chain_of[kind, half, t]
                    if kind == "qi" and t == 0:
                        pe.wait_ge(wiT_ready, 1)
                        for b in range(TB):
                            last = pe.transpose(t_bank[:, b * IH:(b + 1) * IH], wiT[:, b * P:(b + 1) * P],
                                                ident[0:IH, 0:IH])
                        last.then_inc(t_ready, 1)
                    if kind in ("k", "q"):
                        for _ in range(3):
                            idx_scores(idx)
                            idx += 1
                    for s in slots_at.get((kind, half, t), ()):
                        slot(s)

            for i in range(TB + MB, len(NORMS)):
                turn_norm(i)
            pe.wait_ge(n_lo, 2 * len(NORMS))

            with pe.Fori(0, FT // 2) as it:
                for q in range(4):
                    if q % 2 == 0:
                        panel_there(it * 2 + (UP0 + q // 2))
                    w = panel(q // 2, KD)
                    pe.wait_ge(bank_read["dve"], it * 4 + (DVE_USES - 3 + q))
                    for k in range(KD):
                        last = product(banks[(N_USES + q) % 4][:, :], [a[:, k, (q % 2) * P:(q % 2 + 1) * P] for a in w],
                                       [xn2_hi[:, k, :], xn2_lo[:, k, :]], k == 0, k == KD - 1)
                    last.then_inc(bank_ready, 1)
                    if q % 2 == 1:
                        pe.wait_ge(bank_ready, it * 4 + (N_USES + q + 1))
                        pe.sem_inc(panel_used, 1)

            def down(d, slot, start=False, stop=False):
                panel_there(d + DOWN0)
                pe.wait_ge(h_lo, d * 2 + 2)
                w = panel(slot, 2)
                for n in range(8):
                    b, half = n // 2, n % 2
                    for c in range(2):
                        last = product(banks[n][:, :], [a[:, 2 * slot + c, b * P:(b + 1) * P] for a in (xn2_hi, xn2_lo)],
                                       [a[:, c, half * 512:half * 512 + 512] for a in w],
                                       start and c == 0, stop and c == 1)
                    if stop:
                        last.then_inc(bank_ready, 1)
                if not stop:
                    last.then_inc(panel_used, 1)

            pe.wait_ge(bank_read["dve"], DVE_USES + 2 * FT)
            down(0, 0, start=True)
            with pe.Fori(0, (N_DOWN - 3) // 2) as it:
                down(it * 2 + 1, 1)
                down(it * 2 + 2, 0)
            down(N_DOWN - 2, 1)
            down(N_DOWN - 1, 0, stop=True)


INPUTS = ["x", "mem", "g_mix", "w_in", "conv_a_w", "w_a_out", "q_norm_g", "k_norm_g", "w_b_out", "g_mem", "w_mem_kv",
          "mq_norm_g", "mk_norm_g", "w_m_out", "w_o", "g_ffn", "w_up", "conv_f_w", "w_down"]


def kernel(**inputs):
    import numpy as np
    import concourse.bacc as bacc
    from concourse.bass_utils import run_bass_kernel_spmd

    nc = bacc.Bacc("TRN2", target_bir_lowering=False, num_devices=1)
    arrays, args = {}, []
    for name in INPUTS:
        a = np.ascontiguousarray(inputs[name])
        arrays["in_" + name] = a
        args.append(nc.dram_tensor("in_" + name, a.shape, mybir.dt.from_np(a.dtype), kind="ExternalInput").ap())
    args.append(nc.dram_tensor("layer_out", (1, T, D), F32, kind="ExternalOutput").ap())
    hybrid_layer(nc, *args)
    return run_bass_kernel_spmd(nc, [arrays], core_ids=[0]).results[0]["layer_out"]
```

```python
from contextlib import ExitStack

import concourse.bass as bass
from concourse import mybir

F32 = mybir.dt.float32
F32R = mybir.dt.float32r
ALU = mybir.AluOpType
ACT = mybir.ActivationFunctionType
AX = mybir.AxisListType

P = 128
D = 1024
T = 512
M = 256
KD = D // P
TB = T // P
MB = M // P
SC = D // 2
AW = 512
HD = 64
IH, ID = 8, 32
MHD = 128
FF = 2816
FT = FF // P
TOPK = 128
EPS = 1e-6
PANEL = 2048
COLS = PANEL // KD
FILL = -3.0e38
FAR = 1e32

C_B, C_C, C_H, C_Q, C_K, C_V = (i * 512 for i in range(6))
C_KI = C_V + 512 + IH * ID
C_QI = C_V + 512
C_QM = C_KI + ID + IH
C_GATE = C_QM + 512


def hybrid_layer(nc, x, mem, g_mix, w_in, conv_a_w, w_a_out, q_norm_g, k_norm_g, w_b_out, g_mem, w_mem_kv,
                 mq_norm_g, mk_norm_g, w_m_out, w_o, g_ffn, w_up, conv_f_w, w_down, out):
    kxn = lambda w: w[0].rearrange("(k p) n -> p k n", p=P)
    win, wkv, wup, wdown, wo = kxn(w_in), kxn(w_mem_kv), kxn(w_up), kxn(w_down), kxn(w_o)
    wide = lambda w, c: w[:, :, c:c + COLS]
    halves = lambda kind, base, w: [(kind, half, wide(w, base + half * COLS)) for half in range(2)]
    panels = halves("k", C_K, win)
    panels += [("ki", 0, win[:, :, C_KI:C_KI + ID + IH]), ("qi", 0, wide(win, C_QI))]
    for kind, base, w in (("q", C_Q, win), ("v", C_V, win), ("qm", C_QM, win), ("km", 0, wkv), ("vm", AW, wkv)):
        panels += halves(kind, base, w)
    for half in range(2):
        panels += [(kind, half, wide(win, base + half * COLS)) for kind, base in (("c", C_C), ("h", C_H), ("b", C_B))]
    BRANCHES = (("a", 0, kxn(w_a_out)), ("m", 2, kxn(w_m_out)), ("y", 1, kxn(w_b_out)))
    for name, gate, w in BRANCHES:
        gates = [("g" + name, i, wide(win, C_GATE + gate * D + i * COLS)) for i in range(4)]
        outs = [("w" + name, i, w[:, :, i * 512:(i + 1) * 512]) for i in range(2)]
        panels += gates + outs if name == "y" else gates[:2] + outs[:1] + gates[2:] + outs[1:]
    for half in range(2):
        for kh in range(2):
            panels.append(("wo", 2 * half + kh, wo[:, 4 * kh:4 * kh + 4, half * 512:half * 512 + 512]))
    N_HEAD = len(panels)
    N_UP = 2 * FT * P // COLS
    N_DOWN = FT // 2
    UP0, DOWN0 = N_HEAD, N_HEAD + N_UP
    assert UP0 % 2 == 0 and DOWN0 % 2 == 0

    use_of = {}
    last_reader = []

    def uses(key, reader):
        use_of[key] = len(last_reader)
        last_reader.append(reader)

    per_panel = {"ki": (1, "act"), "qi": (2, "act"), "k": (2, "dve"), "q": (2, "dve"), "v": (2, "act"),
                 "qm": (2, "dve"), "km": (1, "dve"), "vm": (1, "act"), "c": (2, "act"), "h": (2, "dve"),
                 "b": (2, "dve"), "g": (2, "act"), "w": (4, "dve")}
    tiles_of = lambda kind: per_panel[kind if kind in per_panel else kind[0]]
    NORMS = [("x", b) for b in range(TB)] + [("mem", b) for b in range(MB)] + [("x2", b) for b in range(TB)]
    turned_before = {("qm", half, t): (TB + half, t) for half in range(MB) for t in range(2)}
    ASIDE = [(i, h) for i in range(2, 10) for h in range(2)]
    for kind, half, _ in panels:
        for t in range(tiles_of(kind)[0]):
            if (kind, half, t) == ("k", 0, 0):
                for i in range(2):
                    for h in range(2):
                        uses(("turn", i, h), "dve")
            if kind != "wo" or half % 2 == 0:
                uses((kind, half, t), tiles_of(kind)[1])
    N_USES = len(last_reader)
    assert last_reader[-4:] == ["dve"] * 4
    DVE_USES = last_reader.count("dve")

    IDX = [(b, h) for b in range(1, TB) for h in range(IH)]
    UNITS = [("m", h, b) for h in range(4) for b in range(TB)]
    UNITS += [("s", h, b) for hp in range(4) for h in (2 * hp, 2 * hp + 1) for b in range(TB)]
    N_UNITS = len(UNITS)
    score_reader = ["act"] * len(IDX) + ["exp" if u[0] == "m" else "dve" for u in UNITS]
    N_CHAINS = 14
    PT0 = 1 + N_CHAINS
    keys = lambda kind, b: M if kind == "m" else (b + 1) * P
    group_end = {u: g for g, u in enumerate([3, 7, 11, 15, 23, 31, 39, 47])}
    group_start = {0: 0, 4: 1, 8: 2, 12: 3, 16: 4, 24: 5, 32: 6, 40: 7}

    N_SLOTS = N_UNITS + 4
    slots_at, s = {}, 0
    for kind, half, _ in panels:
        if kind in ("c", "h", "b", "ga", "wa", "gm", "wm", "gy"):
            for t in range(tiles_of(kind)[0]):
                slots_at[kind, half, t] = range(s, min(s + (2 if s == 0 else 1), N_SLOTS))
                s = slots_at[kind, half, t].stop
    assert s == N_SLOTS

    with ExitStack() as ctx:
        names = []

        def sb(name, shape, dt=F32, stack=ctx):
            return stack.enter_context(nc.sbuf_tensor(name, shape, dt))

        def sem(name):
            return ctx.enter_context(nc.semaphore(name))

        def shared(stack, *lives):
            made = []
            for n, life in enumerate(lives):
                with ExitStack() as own:
                    made.append([sb(name, shape, dt, own) for name, shape, dt in life])
                    if n == len(lives) - 1:
                        stack.push(own.pop_all())
            return made

        ident = sb("ident", [P, P])
        cst = sb("cst", [P, 3 * 2 * FT + 44])
        raw = [sb(f"raw{i}", [P, PANEL]) for i in range(2)]
        whi = [sb(f"whi{i}", [P, PANEL], F32R) for i in range(2)]
        wlo = [sb(f"wlo{i}", [P, PANEL], F32R) for i in range(2)]
        xn_hi = sb("xn_hi", [P, KD, T], F32R)
        xn_lo = sb("xn_lo", [P, KD, T], F32R)
        m_half = sb("m_half", [P, 8])
        stats = sb("stats", [P, 64])
        n_ss, n_ms, n_rs = (stats[:, 10 * i:10 * i + 10] for i in range(3))
        e_max, e_sum, e_inv, n_ss1, n_ms1 = (stats[:, 32 + 4 * i:36 + 4 * i] for i in range(5))
        c_stats = sb("c_stats", [P, 2, 24])
        wi = sb("wi", [P, TB * IH])

        first = ExitStack()
        early = first
        (x_tok,), (ya_hi, ya_lo), (t_y,) = shared(
            early, [("x_tok", [P, TB, D], F32)],
            [("ya_hi", [P, 4, T], F32R), ("ya_lo", [P, 4, T], F32R)], [("t_y", [P, KD, T], F32)])
        (memn_hi, memn_lo), (ym_hi, ym_lo) = shared(
            early, [("memn_hi", [P, KD, M], F32R), ("memn_lo", [P, KD, M], F32R)],
            [("ym_hi", [P, 4, T], F32R), ("ym_lo", [P, 4, T], F32R)])
        (mem_tok,), (cbuf, cvbuf), (t_am,) = shared(
            early, [("mem_tok", [P, MB, D], F32)], [("cbuf", [P, 2, T], F32), ("cvbuf", [P, 2, T], F32)],
            [("t_am", [P, 4, T], F32)])
        (sq, qn, wiT, rl, nt), (merged,) = shared(
            early, [("sq", [P, T], F32), ("qn", [P, 2, T], F32), ("wiT", [IH, T], F32), ("rl", [P, 2, T], F32),
                    ("nt", [P, 2, T], F32)],
            [("merged", [P, KD, T], F32)])
        qT = sb("qT", [P, 4, T], F32, early)
        kT = sb("kT", [P, 4, T], F32, early)
        v = sb("v", [P, TB, AW], F32, early)
        (stage_a, stage_b), (qmT, kmT, vm), (yb_hi, yb_lo) = shared(
            early, [("stage_a", [2 * FT, 3, P], F32), ("stage_b", [40, P], F32)], [("qmT", [P, 4, T], F32), ("kmT", [P, 4, M], F32),
                                                                   ("vm", [P, MB, AW], F32)],
            [("yb_hi", [P, 4, T], F32R), ("yb_lo", [P, 4, T], F32R)])
        (qiT, kiT), (prob, probT) = shared(
            early, [("qiT", [P, 2, T], F32), ("kiT", [P, T], F32)],
            [("prob", [P, 4, T], F32), ("probT", [P, 2, T], F32)])
        offset = {1: 0, 2: 256, 3: 640}
        score = sb("score", [P, 1152], F32, early)
        work = sb("work", [P, 1152], F32, early)
        m8 = sb("m8", [P, 8], F32, early)
        far = [sb(f"far{b}", [P, (b + 1) * P], F32, early) for b in range(TB)]
        causal = sb("causal", [P, P], F32, early)
        first.close()
        second = ctx
        x2 = sb("x2", [P, TB, D], F32, second)
        xs2 = sb("xs2", [P, TB, D], F32, second)
        xn2_hi = sb("xn2_hi", [P, KD, T], F32R, second)
        xn2_lo = sb("xn2_lo", [P, KD, T], F32R, second)
        hraw = sb("hraw", [P, FT, T], F32, second)
        taps = sb("taps", [P, 4, T], F32, second)
        nt2 = taps[:, 2:4, :]

        banks = [ctx.enter_context(nc.psum_tensor(f"bank{i}", [P, T], F32)) for i in range(8)]
        s_bank, t_bank, o_bank = banks[4:6], banks[6], banks[7]

        x_landed = [sem(f"x_landed{i}") for i in range(TB)]
        mem_landed, small_landed, x2_landed, stored = sem("mem_landed"), sem("small_landed"), sem("x2_landed"), sem("stored")
        raw_landed = [sem("raw_landed0"), sem("raw_landed1")]
        hi_done, lo_done = sem("hi_done"), sem("lo_done")
        wo_used, down_used = sem("wo_used"), sem("down_used")
        aside_turned, aside_gained = sem("aside_turned"), sem("aside_gained")
        bank_ready = sem("bank_ready")
        bank_read = {"act": sem("bank_read_act"), "dve": sem("bank_read_dve")}
        pool_const, cst_ready, cst_done = sem("pool_const"), sem("cst_ready"), sem("cst_done")
        half_sum = sem("norm_half_sum")
        n_sum, n_mean, n_rstd, n_scaled, n_hi, n_lo = (sem(f"norm_{s}") for s in ("sum", "mean", "rstd", "scaled", "hi", "lo"))
        c_sq, c_mean, c_rstd = sem("chain_sq"), sem("chain_mean"), sem("chain_rstd")
        t_ready, t_read = sem("turned"), sem("turned_read")
        s_ready = sem("score_ready")
        s_read = {"act": sem("score_read_act"), "dve": sem("score_read_dve")}
        ki_ready, qi_ready, wiT_ready, rl_used = sem("ki_ready"), sem("qi_ready"), sem("wiT_ready"), sem("rl_used")
        v_ready, vm_ready = sem("v_ready"), sem("vm_ready")
        max_done, exp_done, prob_done, o_ready, o_hi, o_lo = (sem(s) for s in ("max_done", "exp_done", "prob_done", "o_ready", "o_hi", "o_lo"))
        conv_done, ya_hi_done, ya_lo_done = sem("conv_done"), sem("ya_hi_done"), sem("ya_lo_done")
        t_used, merged_done, mg_hi, mg_lo = sem("gate_used"), sem("merged_done"), sem("mg_hi"), sem("mg_lo")
        tap_done, tap_step, silu_done, pair_done = sem("tap_done"), sem("tap_step"), sem("silu_done"), sem("pair_done")
        h_hi, h_lo, out_done = sem("h_hi"), sem("h_lo"), sem("out_done")
        dve_step = sem("dve_step")

        tap_f = lambda tap, tile: tap * 2 * FT + tile
        G0 = 3 * 2 * FT
        col = lambda i: cst[:, i:i + 1]
        g_cols = {"x": G0, "mem": G0 + 8, "x2": G0 + 16}
        tap_a = lambda tap, tile: G0 + 24 + tap * 4 + tile
        gain = {"k": G0 + 37, "km": G0 + 39, "q": G0 + 40, "qm": G0 + 41}

        def count(readers, who, upto):
            return readers[:upto + 1].count(who)

        def panel(slot, k):
            return [w[slot][:, :].rearrange("p (k n) -> p k n", k=k) for w in (whi, wlo)]

        def small_panel(slot, k, n):
            return [w[slot][:, 0:k * n].rearrange("p (k n) -> p k n", k=k) for w in (whi, wlo)]

        def norm_place(i):
            kind, b = NORMS[i]
            src = {"x": x_tok, "mem": mem_tok, "x2": x2}[kind][:, b, :]
            dst = {"x": x_tok, "mem": mem_tok, "x2": xs2}[kind][:, b, :]
            hi, lo = {"x": (xn_hi, xn_lo), "mem": (memn_hi, memn_lo), "x2": (xn2_hi, xn2_lo)}[kind]
            tmp = [nt2[:, h, :] if kind == "x2" else nt[:, h, :] for h in range(2)]
            return kind, b, src, dst, hi, lo, tmp

        def norm_bank(i, half):
            if (i, half) in ASIDE:
                if NORMS[i][0] == "mem":
                    return o_bank
                return banks[4 + half] if i < TB else banks[4 + (2 * NORMS[i][1] + half) % 4]
            return banks[use_of["turn", i, half] % 4]

        def wait_turned(eng, i, half):
            if (i, half) in ASIDE:
                eng.wait_ge(aside_turned, ASIDE.index((i, half)) + 1)
            else:
                eng.wait_ge(bank_ready, use_of["turn", i, half] + 1)

        def wait_gained(eng, i, half):
            if (i, half) in ASIDE:
                eng.wait_ge(aside_gained, ASIDE.index((i, half)) + 1)
            else:
                eng.wait_ge(bank_read["dve"], count(last_reader, "dve", use_of["turn", i, half]))

        def wait_used(eng, p):
            kind, half, _ = panels[p]
            if kind == "wo" and half % 2 == 0:
                eng.wait_ge(wo_used, half // 2 + 1)
            else:
                eng.wait_ge(bank_ready, use_of[kind, half - (half % 2 if kind == "wo" else 0), tiles_of(kind)[0] - 1] + 1)

        CHAINS = [(kind, half, i) for kind in ("k", "q", "qm", "km") for half in range(2)
                  for i in range(1 if kind == "km" else 2)]
        assert len(CHAINS) == N_CHAINS
        chain_of = {c: n for n, c in enumerate(CHAINS)}
        WI_TURN = 4
        turn_of = lambda c: c if c < WI_TURN else c + 1

        def chain_shape(kind):
            g = HD if kind in "qk" else MHD
            return g, T // g

        chain_dst = {"k": kT, "q": qT, "qm": qmT, "km": kmT}
        gate_slot = lambda g: t_am[:, g % 4, :] if g < 16 else t_y[:, g - 16, :]

        block = ctx.enter_context(nc.Block())

        @block.sync
        def _(sp):
            for b in range(TB):
                sp.dma_start(x_tok[:, b, :], x[0, b * P:(b + 1) * P, :]).then_inc(x_landed[b], 16)

            for r, g in ((0, g_mix), (8, g_mem), (16, g_ffn)):
                sp.dma_start(stage_b[r:r + 8, :], g[0].rearrange("(k p) -> k p", p=P)).then_inc(small_landed, 16)
            for tap in range(3):
                sp.dma_start(stage_b[24 + 4 * tap:28 + 4 * tap, :],
                             conv_a_w[0, tap].rearrange("(k p) -> k p", p=P)).then_inc(small_landed, 16)
            for r, g in enumerate((q_norm_g, k_norm_g)):
                for h in range(2):
                    sp.dma_start(stage_b[36 + r:37 + r, h * HD:(h + 1) * HD], g).then_inc(small_landed, 16)
            for r, g in enumerate((mq_norm_g, mk_norm_g)):
                sp.dma_start(stage_b[38 + r:39 + r, :], g).then_inc(small_landed, 16)
            sp.dma_start(stage_a[:, :, :], conv_f_w[0].rearrange("t (j p) -> j t p", p=P)).then_inc(small_landed, 16)

            def slot_free(p):
                sp.wait_ge(lo_done, 2 * (p - 1))

            for p, (_, _, src) in enumerate(panels):
                if p == 2:
                    sp.dma_start(mem_tok[:, :, :], mem[0].rearrange("(b p) d -> p b d", p=P)).then_inc(mem_landed, 16)
                if p >= 2:
                    slot_free(p)
                k, n = src.shape[1:]
                dst = raw[p % 2][:, 0:k * n].rearrange("p (k n) -> p k n", k=k)
                sp.dma_start(dst, src).then_inc(raw_landed[p % 2], 16)
            with sp.Fori(0, FT // 2) as it:
                for s in range(2):
                    slot_free(it * 2 + (UP0 + s))
                    sp.dma_start(raw[s][:, :].rearrange("p (k n) -> p k n", k=KD),
                                 wup[:, :, bass.ds(it * COLS + s * FF, COLS)]).then_inc(raw_landed[s], 16)
            for d in range(N_DOWN):
                slot_free(DOWN0 + d)
                sp.dma_start(raw[d % 2][:, :].rearrange("p (k n) -> p k n", k=2),
                             wdown[:, 2 * d:2 * d + 2, :]).then_inc(raw_landed[d % 2], 16)
            for n in range(8):
                b, half = n // 2, n % 2
                sp.wait_ge(out_done, n + 1)
                sp.dma_start(out[0, b * P:(b + 1) * P, half * 512:half * 512 + 512],
                             x2[:, b, half * 512:half * 512 + 512]).then_inc(stored, 16)
            sp.wait_ge(stored, 8 * 16)

        @block.gpsimd
        def _(pool):
            pool.memset(ident[:, :], 0.0).then_inc(pool_const, 1)
            pool.wait_ge(pool_const, 1)
            pool.affine_select(out=ident[:, :], in_=ident[:, :], compare_op=ALU.not_equal, fill=1.0, base=0,
                               pattern=[[-1, P]], channel_multiplier=1).then_inc(pool_const, 1)
            pool.memset(m_half[:, :], -0.5).then_inc(pool_const, 1)
            pool.wait_ge(pool_const, 3)

            def norm_rstd(i):
                pool.wait_ge(n_mean, i + 1)
                pool.tensor_tensor(n_rs[:, i:i + 1], n_ms[:, i:i + 1], m_half[:, 0:1], ALU.pow).then_inc(n_rstd, 1)

            for i in range(TB):
                norm_rstd(i)
            for b in range(TB):
                pool.iota(far[b][:, :], pattern=[[-1, (b + 1) * P]], base=b * P, channel_multiplier=1,
                          allow_small_or_imprecise_dtypes=True).then_inc(pool_const, 1)
            pool.memset(causal[:, :], 0.0).then_inc(pool_const, 1)
            pool.wait_ge(pool_const, 4 + TB)
            pool.affine_select(out=far[0][:, :], in_=far[0][:, :], compare_op=ALU.is_ge, fill=FAR, base=0,
                               pattern=[[-1, P]], channel_multiplier=1).then_inc(pool_const, 1)
            pool.affine_select(out=causal[:, :], in_=causal[:, :], compare_op=ALU.is_ge, fill=-1e38, base=0,
                               pattern=[[-1, P]], channel_multiplier=1).then_inc(pool_const, 1)

            def chain_rstd(c):
                _, n = chain_shape(CHAINS[c][0])
                pool.wait_ge(c_mean, c + 1)
                pool.tensor_tensor(c_stats[:, c % 2, 16:16 + n], c_stats[:, c % 2, 8:8 + n], m_half[:, 0:n],
                                   ALU.pow).then_inc(c_rstd, 1)

            for c in range(4):
                chain_rstd(c)
            for i in range(TB, TB + MB):
                norm_rstd(i)
            for c in range(4, N_CHAINS):
                chain_rstd(c)
            pool.wait_ge(merged_done, KD)
            for b in range(TB):
                pool.dma_start(x2[:, b, :], x[0, b * P:(b + 1) * P, :]).then_inc(x2_landed, 16)
            for i in range(TB + MB, len(NORMS)):
                norm_rstd(i)

        @block.scalar
        def _(act):
            def split_hi(n, slot):
                for piece in range(2):
                    sl = slice(piece * n // 2, (piece + 1) * n // 2)
                    act.activation(whi[slot][:, sl], raw[slot][:, sl], ACT.Copy).then_inc(hi_done, 1)

            def split_head(p):
                if p >= 2:
                    wait_used(act, p - 2)
                act.wait_ge(raw_landed[p % 2], 16 * (p // 2 + 1))
                n = panels[p][2].shape[1] * panels[p][2].shape[2] if p < N_HEAD else PANEL
                split_hi(n, p % 2)

            def norm_sum(i):
                kind, b, src, dst, *_ = norm_place(i)
                if kind == "x":
                    act.wait_ge(x_landed[b], 16)
                elif kind == "mem":
                    act.wait_ge(mem_landed, 16)
                else:
                    act.wait_ge(bank_read["dve"], count(last_reader, "dve", use_of["wo", 2, b]))
                if i >= 1:
                    act.wait_ge(n_sum, i)
                scratch = {"x": score[:, 0:D], "mem": qmT[:, 0:2, :].rearrange("p a t -> p (a t)"),
                           "x2": xs2[:, b, 512:D]}[kind]
                if kind == "x2":
                    src = src[:, 512:D]
                act.activation(scratch, src, ACT.Square, accum_out=n_ss[:, i:i + 1]).then_inc(n_sum, 1)

            def residual_sum(b):
                act.wait_ge(bank_read["dve"], count(last_reader, "dve", use_of["wo", 0, b]))
                act.activation(xs2[:, b, 0:512], x2[:, b, 0:512], ACT.Square, accum_out=n_ss1[:, b:b + 1])\
                   .then_inc(half_sum, 1)

            def residual_scale(b):
                i = TB + MB + b
                act.wait_ge(half_sum, b + 1)
                act.wait_ge(n_sum, i + 1)
                act.wait_ge(n_rstd, i + 1)
                act.activation(xs2[:, b, :], x2[:, b, :], ACT.Copy, scale=n_rs[:, i:i + 1]).then_inc(n_scaled, 1)

            def norm_hi(i, half):
                kind, b, src, dst, hi, lo, tmp = norm_place(i)
                wait_gained(act, i, half)
                act.activation(hi[:, 4 * half:4 * half + 4, b * P:(b + 1) * P],
                               tmp[half].rearrange("p (k t) -> p k t", k=4), ACT.Copy).then_inc(n_hi, 1)

            def chain_square(c, use):
                act.wait_ge(bank_ready, use + 1)
                if c >= 1:
                    act.wait_ge(c_mean, c)
                act.activation(sq[:, :], banks[use % 4][:, :], ACT.Square).then_inc(c_sq, 1)

            def chain_gain(c):
                kind, half, i = CHAINS[c]
                act.wait_ge(t_ready, turn_of(c) + 1)
                act.wait_ge(cst_done, 1)
                dst = chain_dst[kind][:, 2 * half:2 * half + 2, 2 * i * P:2 * i * P + 2 * P]
                act.activation(dst, t_bank[:, :].rearrange("p (c t) -> p c t", c=2), ACT.Copy,
                               scale=col(gain[kind])).then_inc(t_read, 1)

            def idx_relu(u):
                act.wait_ge(s_ready, u + 1)
                if u >= 2:
                    act.wait_ge(rl_used, u - 1)
                b, _ = IDX[u]
                n = (b + 1) * P
                act.activation(rl[:, u % 2, 0:n], s_bank[u % 2][:, 0:n], ACT.Relu).then_inc(s_read["act"], 1)

            def slot(s):
                if 0 <= s - 3 < N_UNITS:
                    u = s - 3
                    kind, h, b = UNITS[u]
                    act.wait_ge(t_ready, PT0 + u + 1)
                    if u >= 2:
                        act.wait_ge(o_ready, u - 1)
                    n = keys(kind, b)
                    act.activation(probT[:, u % 2, 0:n], t_bank[:, 0:n], ACT.Copy).then_inc(t_read, 1)
                if s - 4 in group_end:
                    g = group_end[s - 4]
                    act.wait_ge(o_ready, s - 3)
                    dst = ym_hi[:, g, :] if g < 4 else yb_hi[:, g - 4, :]
                    act.activation(dst, o_bank[:, :], ACT.Copy).then_inc(o_hi, 1)
                if s < N_UNITS:
                    kind, h, b = UNITS[s]
                    n = keys(kind, b)
                    act.wait_ge(max_done, s + 1)
                    if kind == "m" and s >= 4:
                        act.wait_ge(t_ready, PT0 + s - 3)
                    src = s_bank[(len(IDX) + s) % 2][:, 0:n] if kind == "m" else prob[:, s % 4, 0:n]
                    ins = act.activation(prob[:, s % 4, 0:n], src, ACT.Exp, bias=e_max[:, s % 4:s % 4 + 1],
                                         accum_out=e_sum[:, s % 4:s % 4 + 1])
                    ins.then_inc(exp_done, 1)

            def norm_his(*blocks):
                for i in blocks:
                    for half in range(2):
                        norm_hi(i, half)

            for i in range(TB):
                norm_sum(i)
            norm_his(0, 1)
            split_head(0)
            norm_his(2, 3)
            split_head(1)

            pending = None
            idx = 0
            for p, (kind, half, src) in enumerate(panels):
                for t in range(tiles_of(kind)[0]):
                    if kind == "wo":
                        if half == 1:
                            residual_sum(t)
                        elif half == 3:
                            norm_sum(TB + MB + t)
                            residual_scale(t)
                            if t == 2:
                                norm_his(6)
                        continue
                    if (kind, half, t) in turned_before:
                        norm_hi(*turned_before[kind, half, t])
                    n = use_of[kind, half, t]
                    ps = banks[n % 4]
                    if kind in ("k", "q", "qm", "km"):
                        chain_square(chain_of[kind, half, t], n)
                    elif kind == "ki":
                        act.wait_ge(bank_ready, n + 1)
                        act.activation(wiT[:, :], ps[ID:ID + IH, :], ACT.Copy).then_inc(wiT_ready, 1)
                        for r in range(3):
                            act.activation(kiT[r * ID:(r + 1) * ID, :], ps[0:ID, :], ACT.Copy).then_inc(ki_ready, 1)
                        act.activation(kiT[3 * ID:4 * ID, :], ps[0:ID, :], ACT.Copy).then_inc(bank_read["act"], 1)
                    elif kind == "qi":
                        act.wait_ge(bank_ready, n + 1)
                        act.activation(qiT[:, t, :], ps[:, :], ACT.Copy).then_inc(bank_read["act"], 1)
                        if t == 1:
                            act.wait_ge(t_ready, WI_TURN + 1)
                            act.activation(wi[:, :], t_bank[:, 0:TB * IH], ACT.Copy).then_inc(t_read, 1)
                    elif kind in ("v", "vm"):
                        act.wait_ge(bank_ready, n + 1)
                        dst = (v if kind == "v" else vm)[:, 2 * t:2 * t + 2, half * COLS:(half + 1) * COLS]
                        act.activation(dst, ps[:, :].rearrange("p (b n) -> p b n", b=2), ACT.Copy)\
                           .then_inc(bank_read["act"], 1)
                    elif kind == "c":
                        act.wait_ge(bank_ready, n + 1)
                        if half == 1:
                            act.wait_ge(conv_done, t + 1)
                        act.activation(cbuf[:, t, :], ps[:, :], ACT.Copy).then_inc(bank_read["act"], 1)
                    elif kind == "b":
                        act.wait_ge(bank_read["dve"], count(last_reader, "dve", n))
                        act.activation(ya_hi[:, 2 * half + t, :], cvbuf[:, t, :], ACT.Copy).then_inc(ya_hi_done, 1)
                    elif kind[0] == "g":
                        g = {"a": 0, "m": 8, "y": 16}[kind[1]] + 2 * half + t
                        act.wait_ge(bank_ready, n + 1)
                        if 4 <= g < 16:
                            act.wait_ge(t_used, g - 3)
                        act.activation(gate_slot(g), ps[:, :], ACT.Tanh, scale=0.5).then_inc(bank_read["act"], 1)
                    elif kind == "wy":
                        j = 4 * half + t
                        act.wait_ge(merged_done, j + 1)
                        act.activation(xn_hi[:, j, :], merged[:, j, :], ACT.Copy, scale=0.5).then_inc(mg_hi, 1)
                    if pending is not None:
                        chain_gain(pending)
                        pending = None
                    if kind in ("k", "q", "qm", "km"):
                        pending = chain_of[kind, half, t]
                    if kind in ("q", "v", "qm"):
                        for _ in range(2):
                            idx_relu(idx)
                            idx += 1
                    for s in slots_at.get((kind, half, t), ()):
                        slot(s)
                if p == N_HEAD - 1:
                    norm_his(7)
                split_head(p + 2)
                if kind == "qi":
                    for i in range(TB, TB + MB):
                        norm_sum(i)
            norm_his(8, 9)

            def up(it):
                for q in range(4):
                    i = q % 2
                    act.wait_ge(bank_ready, it * 4 + (N_USES + q + 1))
                    act.wait_ge(pair_done, it * 2 + (i + 1))
                    act.activation(taps[:, q, :], banks[(N_USES + q) % 4][:, :], ACT.Copy,
                                   scale=cst[:, bass.ds(it * 2 + tap_f(2, (q // 2) * FT + i), 1)]).then_inc(tap_done, 1)
                    if i == 1:
                        act.wait_ge(raw_landed[q // 2], it * 16 + 16 * ((UP0 + q // 2 + 2) // 2 + 1))
                        split_hi(PANEL, q // 2)
                    if q == 1:
                        for g in range(2):
                            act.wait_ge(bank_read["dve"], it * 4 + (DVE_USES + g + 1))
                            act.activation(taps[:, g, :], taps[:, g, :], ACT.Silu).then_inc(silu_done, 1)

            def split_h_hi(d, slot):
                for c in range(2):
                    act.activation(xn_hi[:, 2 * slot + c, :], hraw[:, bass.ds(d * 2 + c, 1), :].squeeze(1),
                                   ACT.Copy).then_inc(h_hi, 1)

            up(0)
            act.wait_ge(pair_done, 4)
            split_h_hi(0, 0)
            with act.Fori(1, FT // 2) as it:
                up(it)
            act.wait_ge(pair_done, FT + 2)
            split_h_hi(1, 1)

            def down_next(d, slot):
                act.wait_ge(down_used, d + 1)
                act.wait_ge(raw_landed[slot], (d - slot) * 8 + 16 * (DOWN0 // 2 + 2))
                split_hi(PANEL, slot)
                split_h_hi(d + 2, slot)

            down_next(0, 0)
            with act.Fori(0, (N_DOWN - 3) // 2) as it:
                down_next(it * 2 + 1, 1)
                down_next(it * 2 + 2, 0)

        @block.vector
        def _(dve):
            steps = [0]

            def link(ins):
                steps[0] += 1
                ins.then_inc(dve_step, 1)
                dve.wait_ge(dve_step, steps[0])

            def split_lo(slot, n, hi_value):
                for piece in range(2):
                    sl = slice(piece * n // 2, (piece + 1) * n // 2)
                    dve.wait_ge(hi_done, hi_value + (piece + 1))
                    dve.tensor_tensor(wlo[slot][:, sl], raw[slot][:, sl], whi[slot][:, sl], ALU.subtract)\
                       .then_inc(lo_done, 1)

            def split_head(p):
                n = panels[p][2].shape[1] * panels[p][2].shape[2] if p < N_HEAD else PANEL
                split_lo(p % 2, n, 2 * p)

            def norm_mean(i):
                dve.wait_ge(n_sum, i + 1)
                kind, b = NORMS[i]
                if kind == "x2":
                    dve.scalar_tensor_tensor(n_ms[:, i:i + 1], n_ss[:, i:i + 1], 1.0 / D, n_ms1[:, b:b + 1],
                                             ALU.mult, ALU.add).then_inc(n_mean, 1)
                else:
                    dve.tensor_scalar(n_ms[:, i:i + 1], n_ss[:, i:i + 1], 1.0 / D, EPS, ALU.mult, ALU.add)\
                       .then_inc(n_mean, 1)

            def norm_scale(i):
                _, _, src, dst, *_ = norm_place(i)
                dve.wait_ge(n_rstd, i + 1)
                dve.tensor_scalar(dst, src, n_rs[:, i:i + 1], None, ALU.mult).then_inc(n_scaled, 1)

            def norm_gain(i, half):
                kind, b, _, _, hi, lo, tmp = norm_place(i)
                wait_turned(dve, i, half)
                if 2 * i + half >= 2:
                    dve.wait_ge(n_lo, 2 * i + half - 1)
                g0 = g_cols[kind] + 4 * half
                g = cst[:, g0:g0 + 4].unsqueeze(2).to_broadcast([P, 4, P])
                dve.tensor_tensor(tmp[half].rearrange("p (k t) -> p k t", k=4),
                                  norm_bank(i, half)[:, :].rearrange("p (k t) -> p k t", k=4), g,
                                  ALU.mult).then_inc(aside_gained if (i, half) in ASIDE else bank_read["dve"], 1)

            def norm_lo(i, half):
                _, b, _, _, hi, lo, tmp = norm_place(i)
                dve.wait_ge(n_hi, 2 * i + half + 1)
                at = (slice(None), slice(4 * half, 4 * half + 4), slice(b * P, (b + 1) * P))
                dve.tensor_tensor(lo[at], tmp[half].rearrange("p (k t) -> p k t", k=4), hi[at],
                                  ALU.subtract).then_inc(n_lo, 1)

            def norm_turned(*blocks):
                last = None
                for i in blocks:
                    for half in range(2):
                        norm_gain(i, half)
                        if last is not None:
                            norm_lo(*last)
                        last = (i, half)
                norm_lo(*last)

            def chain_stat(c):
                g, n = chain_shape(CHAINS[c][0])
                st = c_stats[:, c % 2, :]
                dve.wait_ge(c_sq, c + 1)
                link(dve.tensor_reduce(st[:, 0:n], sq[:, :].rearrange("p (n g) -> p n g", g=g), AX.X, ALU.add))
                dve.tensor_scalar(st[:, 8:8 + n], st[:, 0:n], 1.0 / g, EPS, ALU.mult, ALU.add).then_inc(c_mean, 1)

            def chain_norm(c, use):
                g, n = chain_shape(CHAINS[c][0])
                dve.wait_ge(c_rstd, c + 1)
                if c >= 2:
                    dve.wait_ge(t_ready, turn_of(c - 2) + 1)
                r = c_stats[:, c % 2, 16:16 + n].unsqueeze(2).to_broadcast([P, n, g])
                dve.tensor_tensor(qn[:, c % 2, :].rearrange("p (n g) -> p n g", g=g),
                                  banks[use % 4][:, :].rearrange("p (n g) -> p n g", g=g), r,
                                  ALU.mult).then_inc(bank_read["dve"], 1)

            def idx_add(u):
                b, h = IDX[u]
                n = (b + 1) * P
                sc = score[:, offset[b]:offset[b] + n]
                w = wi[:, b * IH + h:b * IH + h + 1]
                dve.wait_ge(s_read["act"], u + 1)
                if u == 0:
                    dve.wait_ge(t_read, WI_TURN + 1)
                if h == 0:
                    dve.tensor_scalar(sc, rl[:, u % 2, 0:n], w, 0.0, ALU.mult, ALU.add).then_inc(rl_used, 1)
                else:
                    dve.wait_ge(rl_used, u)
                    dve.scalar_tensor_tensor(sc, rl[:, u % 2, 0:n], w, sc, ALU.mult, ALU.add).then_inc(rl_used, 1)
                if h == IH - 1:
                    dve.wait_ge(rl_used, u + 1)
                    dve.wait_ge(pool_const, 6 + TB)
                    diag = score[:, offset[b] + b * P:offset[b] + n]
                    link(dve.tensor_tensor(diag, diag, causal[:, :], ALU.add))

            def topk_round(r):
                b, r = 1 + r // (TOPK // 8), r % (TOPK // 8)
                n = (b + 1) * P
                sc, wk = score[:, offset[b]:offset[b] + n], work[:, offset[b]:offset[b] + n]
                src = sc if r == 0 else wk
                link(dve.max(m8[:, :], src))
                link(dve.match_replace(wk, m8[:, :], src, FILL))
                if r == TOPK // 8 - 1:
                    link(dve.scalar_tensor_tensor(wk, wk, 1.0, sc, ALU.mult, ALU.is_equal))
                    link(dve.scalar_tensor_tensor(far[b][:, :], wk, FAR, far[b][:, :], ALU.mult, ALU.add))

            def slot(s):
                if 0 <= s - 1 < N_UNITS:
                    u = s - 1
                    kind, h, b = UNITS[u]
                    pr = prob[:, u % 4, 0:keys(kind, b)]
                    dve.wait_ge(exp_done, u + 1)
                    link(dve.reciprocal(e_inv[:, u % 4:u % 4 + 1], e_sum[:, u % 4:u % 4 + 1]))
                    dve.tensor_scalar(pr, pr, e_inv[:, u % 4:u % 4 + 1], None, ALU.mult).then_inc(prob_done, 1)
                if s < N_UNITS:
                    kind, h, b = UNITS[s]
                    n = keys(kind, b)
                    dve.wait_ge(s_ready, len(IDX) + s + 1)
                    ps = s_bank[(len(IDX) + s) % 2][:, 0:n]
                    if kind == "s":
                        slope = 2.0 ** -(h + 1)
                        dve.wait_ge(t_ready, PT0 + s - 3)
                        dve.scalar_tensor_tensor(prob[:, s % 4, 0:n], far[b][:, :], -slope, ps, ALU.mult, ALU.add)\
                           .then_inc(s_read["dve"], 1)
                        dve.wait_ge(s_read["dve"], count(score_reader, "dve", len(IDX) + s))
                        ps = prob[:, s % 4, 0:n]
                    dve.tensor_reduce(e_max[:, s % 4:s % 4 + 1], ps, AX.X, ALU.max, negate=True).then_inc(max_done, 1)
                if s - 4 in group_end:
                    g = group_end[s - 4]
                    hi, lo = (ym_hi, ym_lo) if g < 4 else (yb_hi, yb_lo)
                    dve.wait_ge(o_hi, g + 1)
                    dve.tensor_tensor(lo[:, g % 4, :], o_bank[:, :], hi[:, g % 4, :], ALU.subtract).then_inc(o_lo, 1)

            for i in range(TB):
                norm_mean(i)
                norm_scale(i)
            dve.wait_ge(cst_ready, 1)
            link(dve.tensor_copy(cst[:, 0:G0 + 40], o_bank[:, 0:G0 + 40]))
            link(dve.tensor_scalar(cst[:, G0 + 40:G0 + 41], cst[:, G0 + 36:G0 + 37], HD ** -0.5, None, ALU.mult))
            dve.tensor_scalar(cst[:, G0 + 41:G0 + 42], cst[:, G0 + 38:G0 + 39], MHD ** -0.5, None, ALU.mult)\
               .then_inc(cst_done, 1)
            norm_turned(0, 1)
            split_head(0)
            norm_turned(2, 3)
            split_head(1)

            idx, rounds = 0, 0
            for p, (kind, half, src) in enumerate(panels):
                for t in range(tiles_of(kind)[0] if kind != "wo" or half % 2 == 1 else 0):
                    n = use_of[kind, half - (kind == "wo"), t]
                    ps = banks[n % 4][:, :]
                    if (kind, half, t) in turned_before:
                        norm_gain(*turned_before[kind, half, t])
                    if kind in ("k", "q", "qm", "km"):
                        chain_stat(chain_of[kind, half, t])
                    if kind in ("q", "v", "qm"):
                        for _ in range(2):
                            idx_add(idx)
                            idx += 1
                    if kind in ("v", "qm", "km", "vm", "c", "h", "b"):
                        for _ in range(2):
                            topk_round(rounds)
                            rounds += 1
                    if (kind, half, t) in turned_before:
                        norm_lo(*turned_before[kind, half, t])
                    if kind in ("k", "q", "qm", "km"):
                        chain_norm(chain_of[kind, half, t], n)
                    elif kind == "h":
                        j = 2 * half + t
                        u, cv = cbuf[:, t, :], cvbuf[:, t, :]
                        dve.wait_ge(bank_ready, n + 1)
                        dve.wait_ge(bank_read["act"], count(last_reader, "act", use_of["c", half, t]))
                        if half == 1:
                            dve.wait_ge(ya_lo_done, t + 1)
                        dve.tensor_tensor(u, u, ps, ALU.mult).then_inc(bank_read["dve"], 1)
                        dve.wait_ge(bank_read["dve"], count(last_reader, "dve", n))
                        link(dve.tensor_scalar(cv, u, col(tap_a(2, j)), None, ALU.mult))
                        link(dve.scalar_tensor_tensor(cv[:, 1:T], u[:, 0:T - 1], col(tap_a(1, j)), cv[:, 1:T],
                                                      ALU.mult, ALU.add))
                        dve.scalar_tensor_tensor(cv[:, 2:T], u[:, 0:T - 2], col(tap_a(0, j)), cv[:, 2:T],
                                                 ALU.mult, ALU.add).then_inc(conv_done, 1)
                    elif kind == "b":
                        j = 2 * half + t
                        cv = cvbuf[:, t, :]
                        dve.wait_ge(bank_ready, n + 1)
                        dve.wait_ge(conv_done, j + 1)
                        dve.tensor_tensor(cv, cv, ps, ALU.mult).then_inc(bank_read["dve"], 1)
                        dve.wait_ge(ya_hi_done, j + 1)
                        dve.tensor_tensor(ya_lo[:, j, :], cv, ya_hi[:, j, :], ALU.subtract).then_inc(ya_lo_done, 1)
                    elif kind[0] == "w" and kind != "wo":
                        g = {"a": 0, "m": 8, "y": 16}[kind[1]] + 4 * half + t
                        j = 4 * half + t
                        gt = gate_slot(g)
                        dve.wait_ge(bank_ready, n + 1)
                        dve.wait_ge(bank_read["act"], count(last_reader, "act",
                                                            use_of["g" + kind[1], 2 * half + t // 2, t % 2]))
                        mg = merged[:, j, :]
                        if kind == "wa":
                            dve.scalar_tensor_tensor(mg, gt, 1.0, ps, ALU.add, ALU.mult).then_inc(bank_read["dve"], 1)
                            dve.wait_ge(bank_read["dve"], count(last_reader, "dve", n))
                            dve.sem_inc(t_used, 1)
                        else:
                            dve.scalar_tensor_tensor(gt, gt, 1.0, ps, ALU.add, ALU.mult).then_inc(bank_read["dve"], 1)
                            dve.wait_ge(bank_read["dve"], count(last_reader, "dve", n))
                            done = t_used if kind == "wm" else merged_done
                            dve.tensor_tensor(mg, mg, gt, ALU.add).then_inc(done, 1)
                        if kind == "wy":
                            dve.wait_ge(mg_hi, j + 1)
                            dve.scalar_tensor_tensor(xn_lo[:, j, :], mg, 0.5, xn_hi[:, j, :], ALU.mult,
                                                     ALU.subtract).then_inc(mg_lo, 1)
                    elif kind == "wo":
                        at = x2[:, t, (half // 2) * 512:(half // 2) * 512 + 512]
                        dve.wait_ge(bank_ready, n + 1)
                        dve.wait_ge(x2_landed, 16 * TB)
                        dve.tensor_tensor(at, at, ps, ALU.add).then_inc(bank_read["dve"], 1)
                        if half == 3:
                            norm_mean(TB + MB + t)
                            if t == 2:
                                norm_turned(6)
                    for s in slots_at.get((kind, half, t), ()):
                        slot(s)
                if kind == "wo" and half == 1:
                    dve.wait_ge(half_sum, TB)
                    link(dve.tensor_scalar(n_ms1, n_ss1, 1.0 / D, EPS, ALU.mult, ALU.add))
                if p == N_HEAD - 1:
                    norm_turned(7)
                split_head(p + 2)
                if kind == "qi":
                    for i in range(TB, TB + MB):
                        norm_mean(i)
                        norm_scale(i)
            assert rounds == 3 * TOPK // 8 and idx == len(IDX)
            norm_turned(8, 9)
            dve.wait_ge(n_lo, 2 * len(NORMS))
            dve.sem_inc(pair_done, 2)

            def up(it):
                def hidden(i):
                    dve.wait_ge(silu_done, it * 2 + (i + 1))
                    dve.wait_ge(bank_read["dve"], it * 4 + (DVE_USES + 3 + i))
                    dve.tensor_tensor(hraw[:, bass.ds(it * 2 + i, 1), :].squeeze(1), taps[:, i, :],
                                      taps[:, 2 + i, :], ALU.mult).then_inc(pair_done, 1)

                for q in range(4):
                    i = q % 2
                    tile = (q // 2) * FT + i
                    ps = banks[(N_USES + q) % 4]
                    dve.wait_ge(tap_done, it * 4 + (q + 1))
                    dve.scalar_tensor_tensor(taps[:, q, 1:T], ps[:, 0:T - 1], cst[:, bass.ds(it * 2 + tap_f(1, tile), 1)],
                                             taps[:, q, 1:T], ALU.mult, ALU.add).then_inc(tap_step, 1)
                    dve.wait_ge(tap_step, it * 4 + (q + 1))
                    dve.scalar_tensor_tensor(taps[:, q, 2:T], ps[:, 0:T - 2], cst[:, bass.ds(it * 2 + tap_f(0, tile), 1)],
                                             taps[:, q, 2:T], ALU.mult, ALU.add).then_inc(bank_read["dve"], 1)
                    if i == 1:
                        split_lo(q // 2, PANEL, it * 4 + 2 * (UP0 + q // 2 + 2))
                for i in range(2):
                    hidden(i)

            def split_h_lo(d, slot):
                for c in range(2):
                    dve.wait_ge(h_hi, d * 2 + (c + 1))
                    dve.tensor_tensor(xn_lo[:, 2 * slot + c, :], hraw[:, bass.ds(d * 2 + c, 1), :].squeeze(1),
                                      xn_hi[:, 2 * slot + c, :], ALU.subtract).then_inc(h_lo, 1)

            up(0)
            split_h_lo(0, 0)
            with dve.Fori(1, FT // 2) as it:
                up(it)
            split_h_lo(1, 1)

            def down_next(d, slot):
                split_lo(slot, PANEL, d * 2 + 2 * (DOWN0 + 2))
                split_h_lo(d + 2, slot)

            down_next(0, 0)
            with dve.Fori(0, (N_DOWN - 3) // 2) as it:
                down_next(it * 2 + 1, 1)
                down_next(it * 2 + 2, 0)
            for n in range(8):
                b, half = n // 2, n % 2
                at = x2[:, b, half * 512:half * 512 + 512]
                dve.wait_ge(bank_ready, N_USES + 2 * FT + n + 1)
                dve.tensor_tensor(at, at, banks[n][:, :], ALU.add).then_inc(out_done, 1)

        @block.tensor
        def _(pe):
            def product(o, a, b, start, stop):
                pe.matmul(o, a[0], b[0], start=start, stop=False)
                pe.matmul(o, a[0], b[1], start=False, stop=False)
                return pe.matmul(o, a[1], b[0], start=False, stop=stop)

            def bank_free(n):
                if n >= 4:
                    who = last_reader[n - 4]
                    pe.wait_ge(bank_read[who], count(last_reader, who, n - 4))

            def panel_there(p):
                pe.wait_ge(hi_done, p * 2 + 2)
                pe.wait_ge(lo_done, p * 2 + 2)

            def turn_norm(i, halves=range(2)):
                kind, b, _, dst, *_ = norm_place(i)
                pe.wait_ge(n_scaled, i + 1)
                for half in halves:
                    if (i, half) not in ASIDE:
                        bank_free(use_of["turn", i, half])
                    elif kind == "mem":
                        pe.wait_ge(cst_done, 1)
                        pe.wait_ge(aside_gained, ASIDE.index((i, half)))
                    elif i == 3:
                        pe.wait_ge(aside_gained, ASIDE.index((i, half)) - 1)
                    elif kind == "x2" and b >= 2:
                        pe.wait_ge(aside_gained, ASIDE.index((i, half)) - 3)
                    elif kind == "x2":
                        pe.wait_ge(s_read["dve"], score_reader.count("dve"))
                        pe.wait_ge(t_read, PT0 + N_UNITS)
                        pe.wait_ge(o_lo, 8)
                    for k in range(4):
                        c = (4 * half + k) * P
                        last = pe.transpose(norm_bank(i, half)[:, k * P:(k + 1) * P], dst[:, c:c + P], ident[:, :])
                    last.then_inc(aside_turned if (i, half) in ASIDE else bank_ready, 1)

            def turn_chain(c):
                n = use_of[CHAINS[c]]
                pe.wait_ge(bank_read["dve"], count(last_reader, "dve", n))
                pe.wait_ge(t_read, turn_of(c))
                for cc in range(2):
                    for bb in range(2):
                        last = pe.transpose(t_bank[:, (2 * cc + bb) * P:(2 * cc + bb + 1) * P],
                                            qn[:, c % 2, bb * COLS + cc * P:bb * COLS + (cc + 1) * P], ident[:, :])
                last.then_inc(t_ready, 1)

            def score_bank(k):
                if k >= 2:
                    who = score_reader[k - 2]
                    if who == "exp":
                        pe.wait_ge(exp_done, k - 1 - len(IDX))
                    else:
                        pe.wait_ge(s_read[who], count(score_reader, who, k - 2))
                return s_bank[k % 2]

            def idx_scores(u):
                b, h = IDX[u]
                r = (h % 4) * ID
                ps = score_bank(u)
                if u == 0:
                    pe.wait_ge(bank_read["act"], count(last_reader, "act", use_of["qi", 0, 1]))
                    pe.wait_ge(ki_ready, 3)
                pe.matmul(ps[:, 0:(b + 1) * P], qiT[r:r + ID, h // 4, b * P:(b + 1) * P], kiT[r:r + ID, 0:(b + 1) * P],
                          start=True, stop=True).then_inc(s_ready, 1)

            def slot(s):
                if s < N_UNITS:
                    kind, h, b = UNITS[s]
                    n = keys(kind, b)
                    ps = score_bank(len(IDX) + s)
                    if kind == "m":
                        lhs, rhs = qmT[:, h, b * P:(b + 1) * P], kmT[:, h, :]
                    else:
                        r = (h % 2) * HD
                        lhs, rhs = qT[r:r + HD, h // 2, b * P:(b + 1) * P], kT[r:r + HD, h // 2, 0:n]
                    if s == 0:
                        pe.wait_ge(t_read, PT0)
                    pe.matmul(ps[:, 0:n], lhs, rhs, start=True, stop=True).then_inc(s_ready, 1)
                if 0 <= s - 3 < N_UNITS:
                    u = s - 3
                    kind, h, b = UNITS[u]
                    pe.wait_ge(prob_done, u + 1)
                    pe.wait_ge(t_read, PT0 + u)
                    for j in range(keys(kind, b) // P):
                        last = pe.transpose(t_bank[:, j * P:(j + 1) * P], prob[:, u % 4, j * P:(j + 1) * P], ident[:, :])
                    last.then_inc(t_ready, 1)
                if 0 <= s - 4 < N_UNITS:
                    u = s - 4
                    kind, h, b = UNITS[u]
                    n = keys(kind, b) // P
                    pe.wait_ge(t_read, PT0 + u + 1)
                    if u in group_start and group_start[u] > 0:
                        pe.wait_ge(o_lo, group_start[u])
                    if u == 0:
                        pe.wait_ge(bank_read["act"], count(last_reader, "act", use_of["vm", 1, 0]))
                    for j in range(n):
                        if kind == "m":
                            o, lhs = o_bank[:, b * P:(b + 1) * P], vm[:, j, h * MHD:(h + 1) * MHD]
                        else:
                            r = (h % 2) * HD
                            o, lhs = o_bank[r:r + HD, b * P:(b + 1) * P], v[:, j, h * HD:(h + 1) * HD]
                        last = pe.matmul(o, lhs, probT[:, u % 2, j * P:(j + 1) * P], start=(j == 0), stop=(j == n - 1))
                    last.then_inc(o_ready, 1)

            pe.wait_ge(pool_const, 2)
            turn_norm(0)
            turn_norm(1)
            turn_norm(2)
            pe.wait_ge(small_landed, 16 * 13)
            for tap in range(3):
                pe.transpose(o_bank[:, tap_f(tap, 0):tap_f(tap, 2 * FT)], stage_a[:, tap, :],
                             ident[0:2 * FT, 0:2 * FT])
            pe.transpose(o_bank[:, G0:G0 + 40], stage_b[:, :], ident[0:40, 0:40]).then_inc(cst_ready, 1)
            turn_norm(3)

            pending = None
            idx = 0
            for p, (kind, half, src) in enumerate(panels):
                k_in, cols = src.shape[1:]
                if kind == "km" and half == 0:
                    pe.wait_ge(n_lo, 2 * (TB + MB))
                w = small_panel(p % 2, k_in, cols)
                xn = (xn_hi, xn_lo)
                n_banks = tiles_of(kind)[0]
                for t in range(n_banks):
                    if (kind, half, t) in turned_before:
                        i, h = turned_before[kind, half, t]
                        turn_norm(i, (h,))
                    if t == 0:
                        panel_there(p)
                    if kind == "k" and half == 0:
                        pe.wait_ge(n_lo, 4 * (t + 1))
                    n = use_of[kind, half - half % 2 if kind == "wo" else half, t]
                    ps = banks[n % 4]
                    if kind != "wo" or half % 2 == 0:
                        bank_free(n)
                    if kind in ("k", "q", "v", "qm", "km", "vm"):
                        src_x = (memn_hi, memn_lo) if kind in ("km", "vm") else xn
                        for bb in range(2):
                            tok = slice((2 * t + bb) * P, (2 * t + bb + 1) * P)
                            for k in range(KD):
                                last = product(ps[:, bb * COLS:(bb + 1) * COLS], [a[:, k, tok] for a in src_x],
                                               [a[:, k, :] for a in w], k == 0, k == KD - 1)
                            if bb == 0 and kind in ("q", "v", "qm"):
                                idx_scores(idx)
                                idx += 1
                    elif kind == "wo":
                        kh = half % 2
                        if half < 2 and t == 0:
                            pe.wait_ge(mg_lo, 4 * (half + 1))
                        for k in range(4):
                            last = product(ps[:, :], [a[:, 4 * kh + k, t * P:(t + 1) * P] for a in xn],
                                           [a[:, k, :] for a in w], kh == 0 and k == 0, kh == 1 and k == 3)
                    elif kind[0] == "w":
                        y, there = {"wa": ((ya_hi, ya_lo), (ya_lo_done, 4)), "wm": ((ym_hi, ym_lo), (o_lo, 4)),
                                    "wy": ((yb_hi, yb_lo), (o_lo, 8))}[kind]
                        if kind != "wy":
                            pe.wait_ge(*there)
                        for k in range(4):
                            if kind == "wy":
                                pe.wait_ge(o_lo, 5 + k)
                            last = product(ps[:, :], [a[:, k, t * P:(t + 1) * P] for a in w],
                                           [a[:, k, :] for a in y], k == 0, k == 3)
                    else:
                        m = min(P, cols - t * P)
                        for k in range(KD):
                            last = product(ps[0:m, :], [a[:, k, t * P:t * P + m] for a in w],
                                           [a[:, k, :] for a in xn], k == 0, k == KD - 1)
                    if kind == "wo" and half % 2 == 0:
                        if t == n_banks - 1:
                            last.then_inc(wo_used, 1)
                    else:
                        last.then_inc(bank_ready, 1)
                    if kind == "wo" and half == 3 and t >= 2:
                        turn_norm(TB + MB + t - 2)
                    if pending is not None:
                        turn_chain(pending)
                        pending = None
                    if kind in ("k", "q", "qm", "km"):
                        pending = chain_of[kind, half, t]
                    if kind == "qi" and t == 0:
                        pe.wait_ge(wiT_ready, 1)
                        pe.wait_ge(t_read, WI_TURN)
                        for b in range(TB):
                            last = pe.transpose(t_bank[:, b * IH:(b + 1) * IH], wiT[:, b * P:(b + 1) * P],
                                                ident[0:IH, 0:IH])
                        last.then_inc(t_ready, 1)
                    if kind in ("q", "v", "qm"):
                        idx_scores(idx)
                        idx += 1
                    for s in slots_at.get((kind, half, t), ()):
                        slot(s)

            def up_tile(q, tok):
                w = panel(q // 2, KD)
                for k in range(KD):
                    last = product(banks[(N_USES + q) % 4][:, tok], [a[:, k, (q % 2) * P:(q % 2 + 1) * P] for a in w],
                                   [xn2_hi[:, k, tok], xn2_lo[:, k, tok]], k == 0, k == KD - 1)
                return last

            pe.wait_ge(n_lo, 2 * (TB + MB + 2))
            for q in range(4):
                if q % 2 == 0:
                    panel_there(UP0 + q // 2)
                if q == 2:
                    turn_norm(8)
                    turn_norm(9)
                pe.wait_ge(bank_read["dve"], DVE_USES - 3 + q)
                up_tile(q, slice(0, T // 2))
            pe.wait_ge(n_lo, 2 * len(NORMS))
            for q in range(4):
                up_tile(q, slice(T // 2, T)).then_inc(bank_ready, 1)
            with pe.Fori(1, FT // 2) as it:
                for q in range(4):
                    if q % 2 == 0:
                        panel_there(it * 2 + (UP0 + q // 2))
                    pe.wait_ge(bank_read["dve"], it * 4 + (DVE_USES - 3 + q))
                    up_tile(q, slice(0, T)).then_inc(bank_ready, 1)

            def down(d, slot, start=False, stop=False):
                panel_there(d + DOWN0)
                pe.wait_ge(h_lo, d * 2 + 2)
                w = panel(slot, 2)
                ring = [(N_USES + q) % 4 for q in range(4)]
                for n in [4, 5, 6, 7] + ring if start else range(8):
                    if start and n in ring:
                        pe.wait_ge(bank_read["dve"], DVE_USES + 2 * FT - 3 + ring.index(n))
                    b, half = n // 2, n % 2
                    for c in range(2):
                        last = product(banks[n][:, :], [a[:, 2 * slot + c, b * P:(b + 1) * P] for a in (xn_hi, xn_lo)],
                                       [a[:, c, half * 512:half * 512 + 512] for a in w],
                                       start and c == 0, stop and c == 1)
                    if stop:
                        last.then_inc(bank_ready, 1)
                if not stop:
                    last.then_inc(down_used, 1)

            pe.wait_ge(aside_gained, len(ASIDE))
            down(0, 0, start=True)
            with pe.Fori(0, (N_DOWN - 3) // 2) as it:
                down(it * 2 + 1, 1)
                down(it * 2 + 2, 0)
            down(N_DOWN - 2, 1)
            down(N_DOWN - 1, 0, stop=True)


INPUTS = ["x", "mem", "g_mix", "w_in", "conv_a_w", "w_a_out", "q_norm_g", "k_norm_g", "w_b_out", "g_mem", "w_mem_kv",
          "mq_norm_g", "mk_norm_g", "w_m_out", "w_o", "g_ffn", "w_up", "conv_f_w", "w_down"]


def kernel(**inputs):
    import numpy as np
    import concourse.bacc as bacc
    from concourse.bass_utils import run_bass_kernel_spmd

    nc = bacc.Bacc("TRN2", target_bir_lowering=False, num_devices=1)
    arrays, args = {}, []
    for name in INPUTS:
        a = np.ascontiguousarray(inputs[name])
        arrays["in_" + name] = a
        args.append(nc.dram_tensor("in_" + name, a.shape, mybir.dt.from_np(a.dtype), kind="ExternalInput").ap())
    args.append(nc.dram_tensor("layer_out", (1, T, D), F32, kind="ExternalOutput").ap())
    hybrid_layer(nc, *args)
    return run_bass_kernel_spmd(nc, [arrays], core_ids=[0]).results[0]["layer_out"]
```

```python
from contextlib import ExitStack

import concourse.bass as bass
from concourse import mybir

F32 = mybir.dt.float32
F32R = mybir.dt.float32r
ALU = mybir.AluOpType
ACT = mybir.ActivationFunctionType
AX = mybir.AxisListType

P = 128
D = 1024
T = 512
M = 256
KD = D // P
TB = T // P
MB = M // P
AW = 512
HD = 64
IH, ID = 8, 32
MHD = 128
FF = 2816
FT = FF // P
TOPK = 128
EPS = 1e-6
PANEL = 2048
COLS = PANEL // KD
FILL = -3.0e38
FAR = 1e32

C_B, C_C, C_H, C_Q, C_K, C_V = (i * 512 for i in range(6))
C_KI = C_V + 512 + IH * ID
C_QI = C_V + 512
C_QM = C_KI + ID + IH
C_GATE = C_QM + 512


def hybrid_layer(nc, x, mem, g_mix, w_in, conv_a_w, w_a_out, q_norm_g, k_norm_g, w_b_out, g_mem, w_mem_kv,
                 mq_norm_g, mk_norm_g, w_m_out, w_o, g_ffn, w_up, conv_f_w, w_down, out):
    kxn = lambda w: w[0].rearrange("(k p) n -> p k n", p=P)
    win, wkv, wup, wdown, wo = kxn(w_in), kxn(w_mem_kv), kxn(w_up), kxn(w_down), kxn(w_o)
    wide = lambda w, c: w[:, :, c:c + COLS]
    halves = lambda kind, base, w: [(kind, half, wide(w, base + half * COLS)) for half in range(2)]
    panels = halves("k", C_K, win)
    panels += [("ki", 0, win[:, :, C_KI:C_KI + ID + IH]), ("qi", 0, wide(win, C_QI))]
    for kind, base, w in (("q", C_Q, win), ("v", C_V, win), ("qm", C_QM, win), ("km", 0, wkv), ("vm", AW, wkv)):
        panels += halves(kind, base, w)
    for half in range(2):
        panels += [(kind, half, wide(win, base + half * COLS)) for kind, base in (("c", C_C), ("h", C_H), ("b", C_B))]
    BRANCHES = (("a", 0, kxn(w_a_out)), ("m", 2, kxn(w_m_out)), ("y", 1, kxn(w_b_out)))
    for name, gate, w in BRANCHES:
        gates = [("g" + name, i, wide(win, C_GATE + gate * D + i * COLS)) for i in range(4)]
        outs = [("w" + name, i, w[:, :, i * 512:(i + 1) * 512]) for i in range(2)]
        panels += gates + outs if name == "y" else gates[:2] + outs[:1] + gates[2:] + outs[1:]
    for half in range(2):
        for kh in range(2):
            panels.append(("wo", 2 * half + kh, wo[:, 4 * kh:4 * kh + 4, half * 512:half * 512 + 512]))
    N_HEAD = len(panels)
    N_UP = 2 * FT * P // COLS
    N_DOWN = FT // 2
    UP0, DOWN0 = N_HEAD, N_HEAD + N_UP
    assert UP0 % 2 == 0 and DOWN0 % 2 == 0

    use_of = {}
    last_reader = []

    def uses(key, reader):
        use_of[key] = len(last_reader)
        last_reader.append(reader)

    per_panel = {"ki": (1, "dve"), "qi": (2, "dve"), "k": (2, "dve"), "q": (2, "dve"), "v": (2, "act"),
                 "qm": (2, "dve"), "km": (1, "dve"), "vm": (1, "act"), "c": (2, "act"), "h": (2, "dve"),
                 "b": (2, "dve"), "g": (2, "act"), "w": (4, "dve")}
    tiles_of = lambda kind: per_panel[kind if kind in per_panel else kind[0]]
    NORMS = [("x", b) for b in range(TB)] + [("mem", b) for b in range(MB)] + [("x2", b) for b in range(TB)]
    turned_in = {("v", half, t): (TB + half, t) for half in range(MB) for t in range(2)}
    ASIDE = [(i, h) for i in range(2, len(NORMS)) for h in range(2)]
    for kind, half, _ in panels:
        for t in range(tiles_of(kind)[0]):
            if (kind, half, t) == ("k", 0, 0):
                for i in range(2):
                    for h in range(2):
                        uses(("turn", i, h), "dve")
            if kind != "wo" or half % 2 == 0:
                uses((kind, half, t), tiles_of(kind)[1])
    N_USES = len(last_reader)
    assert last_reader[-4:] == ["dve"] * 4
    DVE_USES = last_reader.count("dve")

    IDX = [(b, h) for b in range(1, TB) for h in range(IH)]
    UNITS = [("m", h, b) for h in range(4) for b in range(TB)]
    UNITS += [("s", h, b) for hp in range(4) for h in (2 * hp, 2 * hp + 1) for b in range(TB)]
    N_UNITS = len(UNITS)
    score_reader = ["act"] * len(IDX) + ["exp" if u[0] == "m" else "dve" for u in UNITS]
    N_CHAINS = 14
    PT0 = 1 + N_CHAINS
    keys = lambda kind, b: M if kind == "m" else (b + 1) * P
    group_end = {u: g for g, u in enumerate([3, 7, 11, 15, 23, 31, 39, 47])}
    group_start = {0: 0, 4: 1, 8: 2, 12: 3, 16: 4, 24: 5, 32: 6, 40: 7}

    N_SLOTS = N_UNITS + 4
    slots_at, s = {}, 0
    for kind, half, _ in panels:
        if kind in ("c", "h", "b", "ga", "wa", "gm", "wm", "gy"):
            for t in range(tiles_of(kind)[0]):
                slots_at[kind, half, t] = range(s, min(s + (2 if s == 0 else 1), N_SLOTS))
                s = slots_at[kind, half, t].stop
    assert s == N_SLOTS

    with ExitStack() as ctx:
        def sb(name, shape, dt=F32, stack=ctx):
            return stack.enter_context(nc.sbuf_tensor(name, shape, dt))

        def sem(name):
            return ctx.enter_context(nc.semaphore(name))

        def shared(stack, *lives):
            made = []
            for n, life in enumerate(lives):
                with ExitStack() as own:
                    made.append([sb(name, shape, dt, own) for name, shape, dt in life])
                    if n == len(lives) - 1:
                        stack.push(own.pop_all())
            return made

        ident = sb("ident", [P, P])
        cst = sb("cst", [P, 3 * 2 * FT + 44])
        raw = [sb(f"raw{i}", [P, PANEL]) for i in range(2)]
        whi = [sb(f"whi{i}", [P, PANEL], F32R) for i in range(2)]
        wlo = [sb(f"wlo{i}", [P, PANEL], F32R) for i in range(2)]
        xn_hi = sb("xn_hi", [P, KD, T], F32R)
        xn_lo = sb("xn_lo", [P, KD, T], F32R)
        m_half = sb("m_half", [P, 8])
        stats = sb("stats", [P, 64])
        n_ss, n_ms, n_rs = (stats[:, 10 * i:10 * i + 10] for i in range(3))
        e_max, e_sum, e_inv, n_ss1, n_ms1 = (stats[:, 32 + 4 * i:36 + 4 * i] for i in range(5))
        c_stats = sb("c_stats", [P, 2, 24])
        wi = sb("wi", [P, TB * IH])

        early = ExitStack()
        (x_tok,), (ya_hi, ya_lo), (t_y,) = shared(
            early, [("x_tok", [P, TB, D], F32)],
            [("ya_hi", [P, 4, T], F32R), ("ya_lo", [P, 4, T], F32R)], [("t_y", [P, KD, T], F32)])
        (memn_hi, memn_lo), (ym_hi, ym_lo) = shared(
            early, [("memn_hi", [P, KD, M], F32R), ("memn_lo", [P, KD, M], F32R)],
            [("ym_hi", [P, 4, T], F32R), ("ym_lo", [P, 4, T], F32R)])
        (mem_tok,), (cbuf, cvbuf), (t_am,) = shared(
            early, [("mem_tok", [P, MB, D], F32)], [("cbuf", [P, 2, T], F32), ("cvbuf", [P, 2, T], F32)],
            [("t_am", [P, 4, T], F32)])
        (sq, qn, wiT, rl, nt), (merged,) = shared(
            early, [("sq", [P, T], F32), ("qn", [P, 2, T], F32), ("wiT", [IH, T], F32), ("rl", [P, 2, T], F32),
                    ("nt", [P, 2, T], F32)],
            [("merged", [P, KD, T], F32)])
        qT = sb("qT", [P, 4, T], F32, early)
        kT = sb("kT", [P, 4, T], F32, early)
        v = sb("v", [P, TB, AW], F32, early)
        (stage_a, stage_b), (qmT, kmT, vm), (yb_hi, yb_lo) = shared(
            early, [("stage_a", [2 * FT, 3, P], F32), ("stage_b", [40, P], F32)],
            [("qmT", [P, 4, T], F32), ("kmT", [P, 4, M], F32), ("vm", [P, MB, AW], F32)],
            [("yb_hi", [P, 4, T], F32R), ("yb_lo", [P, 4, T], F32R)])
        (qi_hi, qi_lo, ki_hi, ki_lo), (prob, probT) = shared(
            early, [("qi_hi", [P, 2, T], F32R), ("qi_lo", [P, 2, T], F32R), ("ki_hi", [P, T], F32R),
                    ("ki_lo", [P, T], F32R)],
            [("prob", [P, 4, T], F32), ("probT", [P, 2, T], F32)])
        offset = {1: 0, 2: 256, 3: 640}
        score = sb("score", [P, 1152], F32, early)
        work = sb("work", [P, 1152], F32, early)
        m8 = sb("m8", [P, 8], F32, early)
        far = [sb(f"far{b}", [P, (b + 1) * P], F32, early) for b in range(TB)]
        causal = sb("causal", [P, P], F32, early)
        early.close()
        x2 = sb("x2", [P, TB, D], F32)
        xs2 = sb("xs2", [P, TB, D], F32)
        xn2_hi = sb("xn2_hi", [P, KD, T], F32R)
        xn2_lo = sb("xn2_lo", [P, KD, T], F32R)
        hraw = sb("hraw", [P, FT, T], F32)
        taps = sb("taps", [P, 4, T], F32)
        nt2 = taps[:, 2:4, :]

        banks = [ctx.enter_context(nc.psum_tensor(f"bank{i}", [P, T], F32)) for i in range(8)]
        s_bank, t_bank, o_bank = banks[4:6], banks[6], banks[7]

        x_landed = [sem(f"x_landed{i}") for i in range(TB)]
        rows_landed = sem("rows_landed")
        narrow_landed, wide_landed = sem("narrow_head_gains_landed"), sem("wide_head_gains_landed")
        mem_landed, x2_landed, stored = sem("mem_landed"), sem("x2_landed"), sem("stored")
        first_landed = sem("first_half_panel_landed")
        raw_landed = [sem("raw_landed0"), sem("raw_landed1")]
        hi_done, lo_done = sem("hi_done"), sem("lo_done")
        wo_used, down_used = sem("wo_used"), sem("down_used")
        aside_turned, aside_gained = sem("aside_turned"), sem("aside_gained")
        bank_ready = sem("bank_ready")
        bank_read = {"act": sem("bank_read_act"), "dve": sem("bank_read_dve")}
        pool_const, cst_ready, cst_done = sem("pool_const"), sem("cst_ready"), sem("cst_done")
        half_sum = sem("norm_half_sum")
        n_sum, n_mean, n_rstd, n_scaled, n_hi, n_lo = (sem(f"norm_{s}") for s in ("sum", "mean", "rstd", "scaled", "hi", "lo"))
        c_sq, c_mean, c_rstd = sem("chain_sq"), sem("chain_mean"), sem("chain_rstd")
        t_ready, t_read = sem("turned"), sem("turned_read")
        s_ready = sem("score_ready")
        s_read = {"act": sem("score_read_act"), "dve": sem("score_read_dve")}
        ki_hi_done, ki_lo_done, qi_hi_done = sem("ki_hi_done"), sem("ki_lo_done"), sem("qi_hi_done")
        wiT_ready, rl_used = sem("wiT_ready"), sem("rl_used")
        max_done, exp_done, prob_done, o_ready, o_hi, o_lo = (sem(s) for s in ("max_done", "exp_done", "prob_done", "o_ready", "o_hi", "o_lo"))
        conv_done, ya_hi_done, ya_lo_done = sem("conv_done"), sem("ya_hi_done"), sem("ya_lo_done")
        t_used, merged_done, mg_hi, mg_lo = sem("gate_used"), sem("merged_done"), sem("mg_hi"), sem("mg_lo")
        tap_done, tap_step, silu_done, pair_done = sem("tap_done"), sem("tap_step"), sem("silu_done"), sem("pair_done")
        h_hi, h_lo, out_done = sem("h_hi"), sem("h_lo"), sem("out_done")
        dve_step = sem("dve_step")

        tap_f = lambda tap, tile: tap * 2 * FT + tile
        G0 = 3 * 2 * FT
        col = lambda i: cst[:, i:i + 1]
        g_cols = {"x": G0, "mem": G0 + 8, "x2": G0 + 16}
        tap_a = lambda tap, tile: G0 + 24 + tap * 4 + tile
        gain = {"k": G0 + 37, "km": G0 + 39, "q": G0 + 40, "qm": G0 + 41}

        def count(readers, who, upto):
            return readers[:upto + 1].count(who)

        def panel(slot, k):
            return [w[slot][:, :].rearrange("p (k n) -> p k n", k=k) for w in (whi, wlo)]

        def small_panel(slot, k, n):
            return [w[slot][:, 0:k * n].rearrange("p (k n) -> p k n", k=k) for w in (whi, wlo)]

        def norm_place(i):
            kind, b = NORMS[i]
            src = {"x": x_tok, "mem": mem_tok, "x2": x2}[kind][:, b, :]
            dst = {"x": x_tok, "mem": mem_tok, "x2": xs2}[kind][:, b, :]
            hi, lo = {"x": (xn_hi, xn_lo), "mem": (memn_hi, memn_lo), "x2": (xn2_hi, xn2_lo)}[kind]
            tmp = [nt2[:, h, :] if kind == "x2" else nt[:, h, :] for h in range(2)]
            return kind, b, src, dst, hi, lo, tmp

        def norm_bank(i, half):
            if (i, half) in ASIDE:
                if NORMS[i][0] == "mem":
                    return o_bank
                return banks[2 * i + half] if i < TB else banks[4 + (2 * NORMS[i][1] + half) % 4]
            return banks[use_of["turn", i, half] % 4]

        def wait_turned(eng, i, half):
            if (i, half) in ASIDE:
                eng.wait_ge(aside_turned, ASIDE.index((i, half)) + 1)
            else:
                eng.wait_ge(bank_ready, use_of["turn", i, half] + 1)

        def wait_gained(eng, i, half):
            if (i, half) in ASIDE:
                eng.wait_ge(aside_gained, ASIDE.index((i, half)) + 1)
            else:
                eng.wait_ge(bank_read["dve"], count(last_reader, "dve", use_of["turn", i, half]))

        def wait_used(eng, p):
            kind, half, _ = panels[p]
            if kind == "wo" and half % 2 == 0:
                eng.wait_ge(wo_used, half // 2 + 1)
            else:
                eng.wait_ge(bank_ready, use_of[kind, half - (half % 2 if kind == "wo" else 0), tiles_of(kind)[0] - 1] + 1)

        CHAINS = [(kind, half, i) for kind in ("k", "q", "qm", "km") for half in range(2)
                  for i in range(1 if kind == "km" else 2)]
        assert len(CHAINS) == N_CHAINS
        chain_of = {c: n for n, c in enumerate(CHAINS)}
        WI_TURN = 4
        turn_of = lambda c: c if c < WI_TURN else c + 1

        def chain_shape(kind):
            g = HD if kind in "qk" else MHD
            return g, T // g

        chain_dst = {"k": kT, "q": qT, "qm": qmT, "km": kmT}
        gate_slot = lambda g: t_am[:, g % 4, :] if g < 16 else t_y[:, g - 16, :]

        block = ctx.enter_context(nc.Block())

        @block.sync
        def _(sp):
            def load_x(b):
                sp.dma_start(x_tok[:, b, :], x[0, b * P:(b + 1) * P, :]).then_inc(x_landed[b], 16)

            def load_half_panel(piece, landed):
                ks = slice(piece * KD // 2, (piece + 1) * KD // 2)
                sp.dma_start(raw[0][:, :].rearrange("p (k n) -> p k n", k=KD)[:, ks, :], panels[0][2][:, ks, :])\
                  .then_inc(landed, 16)

            load_x(0)
            load_half_panel(0, first_landed)
            load_x(1)
            for r, g in ((0, g_mix), (8, g_mem), (16, g_ffn)):
                sp.dma_start(stage_b[r:r + 8, :], g[0].rearrange("(k p) -> k p", p=P)).then_inc(rows_landed, 16)
            sp.dma_start(stage_b[24:36, :], conv_a_w[0].rearrange("t (k p) -> (t k) p", p=P)).then_inc(rows_landed, 16)
            sp.dma_start(stage_a[:, :, :], conv_f_w[0].rearrange("t (j p) -> j t p", p=P)).then_inc(rows_landed, 16)
            load_half_panel(1, raw_landed[0])
            for b in range(2, TB):
                load_x(b)

            def slot_free(p):
                sp.wait_ge(lo_done, 2 * (p - 1))

            for p, (_, _, src) in enumerate(panels):
                if p == 2:
                    sp.dma_start(mem_tok[:, :, :], mem[0].rearrange("(b p) d -> p b d", p=P)).then_inc(mem_landed, 16)
                if p == 0:
                    continue
                if p >= 2:
                    slot_free(p)
                k, n = src.shape[1:]
                dst = raw[p % 2][:, 0:k * n].rearrange("p (k n) -> p k n", k=k)
                sp.dma_start(dst, src).then_inc(raw_landed[p % 2], 16)
            with sp.Fori(0, FT // 2) as it:
                for s in range(2):
                    slot_free(it * 2 + (UP0 + s))
                    sp.dma_start(raw[s][:, :].rearrange("p (k n) -> p k n", k=KD),
                                 wup[:, :, bass.ds(it * COLS + s * FF, COLS)]).then_inc(raw_landed[s], 16)
            for d in range(N_DOWN):
                slot_free(DOWN0 + d)
                sp.dma_start(raw[d % 2][:, :].rearrange("p (k n) -> p k n", k=2),
                             wdown[:, 2 * d:2 * d + 2, :]).then_inc(raw_landed[d % 2], 16)
            for n in range(8):
                b, half = n // 2, n % 2
                sp.wait_ge(out_done, n + 1)
                sp.dma_start(out[0, b * P:(b + 1) * P, half * 512:half * 512 + 512],
                             x2[:, b, half * 512:half * 512 + 512]).then_inc(stored, 16)
            sp.wait_ge(stored, 8 * 16)

        @block.gpsimd
        def _(pool):
            pool.memset(ident[:, :], 0.0).then_inc(pool_const, 1)
            pool.wait_ge(pool_const, 1)
            pool.affine_select(out=ident[:, :], in_=ident[:, :], compare_op=ALU.not_equal, fill=1.0, base=0,
                               pattern=[[-1, P]], channel_multiplier=1).then_inc(pool_const, 1)
            pool.memset(m_half[:, :], -0.5).then_inc(pool_const, 1)
            for r, g in enumerate((mq_norm_g, mk_norm_g)):
                pool.dma_start(stage_b[38 + r:39 + r, :], g).then_inc(wide_landed, 16)
            pool.wait_ge(pool_const, 3)

            def norm_rstd(i):
                pool.wait_ge(n_mean, i + 1)
                pool.tensor_tensor(n_rs[:, i:i + 1], n_ms[:, i:i + 1], m_half[:, 0:1], ALU.pow).then_inc(n_rstd, 1)

            for i in range(TB):
                norm_rstd(i)
            for b in range(TB):
                pool.iota(far[b][:, :], pattern=[[-1, (b + 1) * P]], base=b * P, channel_multiplier=1,
                          allow_small_or_imprecise_dtypes=True).then_inc(pool_const, 1)
            pool.memset(causal[:, :], 0.0).then_inc(pool_const, 1)
            pool.wait_ge(pool_const, 4 + TB)
            pool.affine_select(out=far[0][:, :], in_=far[0][:, :], compare_op=ALU.is_ge, fill=FAR, base=0,
                               pattern=[[-1, P]], channel_multiplier=1).then_inc(pool_const, 1)
            pool.affine_select(out=causal[:, :], in_=causal[:, :], compare_op=ALU.is_ge, fill=-1e38, base=0,
                               pattern=[[-1, P]], channel_multiplier=1).then_inc(pool_const, 1)

            def chain_rstd(c):
                _, n = chain_shape(CHAINS[c][0])
                pool.wait_ge(c_mean, c + 1)
                pool.tensor_tensor(c_stats[:, c % 2, 16:16 + n], c_stats[:, c % 2, 8:8 + n], m_half[:, 0:n],
                                   ALU.pow).then_inc(c_rstd, 1)

            for c in range(4):
                chain_rstd(c)
            for i in range(TB, TB + MB):
                norm_rstd(i)
            for c in range(4, N_CHAINS):
                chain_rstd(c)
            pool.wait_ge(merged_done, KD)
            for b in range(TB):
                pool.dma_start(x2[:, b, :], x[0, b * P:(b + 1) * P, :]).then_inc(x2_landed, 16)
            for i in range(TB + MB, len(NORMS)):
                norm_rstd(i)

        @block.scalar
        def _(act):
            def split_hi(n, slot, pieces=range(2)):
                for piece in pieces:
                    sl = slice(piece * n // 2, (piece + 1) * n // 2)
                    act.activation(whi[slot][:, sl], raw[slot][:, sl], ACT.Copy).then_inc(hi_done, 1)

            def split_head(p):
                if p >= 2:
                    wait_used(act, p - 2)
                act.wait_ge(raw_landed[p % 2], 16 * (p // 2 + 1))
                n = panels[p][2].shape[1] * panels[p][2].shape[2] if p < N_HEAD else PANEL
                split_hi(n, p % 2)

            def norm_sum(i):
                kind, b, src, dst, *_ = norm_place(i)
                if kind == "x":
                    act.wait_ge(x_landed[b], 16)
                elif kind == "mem":
                    act.wait_ge(mem_landed, 16)
                else:
                    act.wait_ge(bank_read["dve"], count(last_reader, "dve", use_of["wo", 2, b]))
                if i >= 1:
                    act.wait_ge(n_sum, i)
                scratch = {"x": score[:, 0:D], "mem": qmT[:, 0:2, :].rearrange("p a t -> p (a t)"),
                           "x2": xs2[:, b, 512:D]}[kind]
                if kind == "x2":
                    src = src[:, 512:D]
                act.activation(scratch, src, ACT.Square, accum_out=n_ss[:, i:i + 1]).then_inc(n_sum, 1)

            def residual_sum(b):
                act.wait_ge(bank_read["dve"], count(last_reader, "dve", use_of["wo", 0, b]))
                act.activation(xs2[:, b, 0:512], x2[:, b, 0:512], ACT.Square, accum_out=n_ss1[:, b:b + 1])\
                   .then_inc(half_sum, 1)

            def norm_rescale(i):
                kind, b, src, dst, *_ = norm_place(i)
                if kind == "x2":
                    act.wait_ge(half_sum, b + 1)
                    act.wait_ge(n_sum, i + 1)
                act.wait_ge(n_rstd, i + 1)
                act.activation(dst, src, ACT.Copy, scale=n_rs[:, i:i + 1]).then_inc(n_scaled, 1)

            def norm_hi(i, half):
                kind, b, src, dst, hi, lo, tmp = norm_place(i)
                wait_gained(act, i, half)
                act.activation(hi[:, 4 * half:4 * half + 4, b * P:(b + 1) * P],
                               tmp[half].rearrange("p (k t) -> p k t", k=4), ACT.Copy).then_inc(n_hi, 1)

            def chain_square(c, use):
                act.wait_ge(bank_ready, use + 1)
                if c >= 1:
                    act.wait_ge(c_mean, c)
                act.activation(sq[:, :], banks[use % 4][:, :], ACT.Square).then_inc(c_sq, 1)

            def chain_gain(c):
                kind, half, i = CHAINS[c]
                act.wait_ge(t_ready, turn_of(c) + 1)
                act.wait_ge(cst_done, 1)
                dst = chain_dst[kind][:, 2 * half:2 * half + 2, 2 * i * P:2 * i * P + 2 * P]
                act.activation(dst, t_bank[:, :].rearrange("p (c t) -> p c t", c=2), ACT.Copy,
                               scale=col(gain[kind])).then_inc(t_read, 1)

            def idx_relu(u):
                act.wait_ge(s_ready, u + 1)
                if u >= 2:
                    act.wait_ge(rl_used, u - 1)
                b, _ = IDX[u]
                n = (b + 1) * P
                act.activation(rl[:, u % 2, 0:n], s_bank[u % 2][:, 0:n], ACT.Relu).then_inc(s_read["act"], 1)

            def slot(s):
                if 0 <= s - 3 < N_UNITS:
                    u = s - 3
                    kind, h, b = UNITS[u]
                    act.wait_ge(t_ready, PT0 + u + 1)
                    if u >= 2:
                        act.wait_ge(o_ready, u - 1)
                    n = keys(kind, b)
                    act.activation(probT[:, u % 2, 0:n], t_bank[:, 0:n], ACT.Copy).then_inc(t_read, 1)
                if s - 4 in group_end:
                    g = group_end[s - 4]
                    act.wait_ge(o_ready, s - 3)
                    dst = ym_hi[:, g, :] if g < 4 else yb_hi[:, g - 4, :]
                    act.activation(dst, o_bank[:, :], ACT.Copy).then_inc(o_hi, 1)
                if s < N_UNITS:
                    kind, h, b = UNITS[s]
                    n = keys(kind, b)
                    act.wait_ge(max_done, s + 1)
                    if kind == "m" and s >= 4:
                        act.wait_ge(t_ready, PT0 + s - 3)
                    src = s_bank[(len(IDX) + s) % 2][:, 0:n] if kind == "m" else prob[:, s % 4, 0:n]
                    act.activation(prob[:, s % 4, 0:n], src, ACT.Exp, bias=e_max[:, s % 4:s % 4 + 1],
                                   accum_out=e_sum[:, s % 4:s % 4 + 1]).then_inc(exp_done, 1)

            def norm_his(*blocks):
                for i in blocks:
                    for half in range(2):
                        norm_hi(i, half)

            for r, g in enumerate((q_norm_g, k_norm_g)):
                act.dma_start(stage_b[36 + r:37 + r, :].rearrange("o (n d) -> o n d", n=2),
                              g.unsqueeze(1).to_broadcast([1, 2, HD])).then_inc(narrow_landed, 16)
            norm_sum(0)
            act.wait_ge(first_landed, 16)
            split_hi(PANEL, 0, [0])
            norm_sum(1)
            norm_his(0)
            act.wait_ge(raw_landed[0], 16)
            split_hi(PANEL, 0, [1])
            norm_sum(2)
            norm_sum(3)
            norm_rescale(2)
            norm_his(1)
            norm_rescale(3)
            norm_his(2, 3)

            pending = None
            idx = 0
            for p, (kind, half, src) in enumerate(panels):
                for t in range(tiles_of(kind)[0]):
                    if kind == "wo":
                        if half == 1:
                            residual_sum(t)
                        elif half == 3:
                            if t == 3:
                                norm_his(TB + MB + 1)
                                split_head(p + 2)
                            norm_sum(TB + MB + t)
                            if t == 2:
                                norm_his(TB + MB)
                            norm_rescale(TB + MB + t)
                        continue
                    if (kind, half, t) in turned_in:
                        norm_hi(*turned_in[kind, half, t])
                    n = use_of[kind, half, t]
                    ps = banks[n % 4]
                    if kind in ("k", "q", "qm", "km"):
                        chain_square(chain_of[kind, half, t], n)
                        if (p, t) == (0, 0):
                            split_head(1)
                    elif kind == "ki":
                        act.wait_ge(bank_ready, n + 1)
                        act.activation(wiT[:, :], ps[ID:ID + IH, :], ACT.Copy).then_inc(wiT_ready, 1)
                        for r in range(4):
                            act.activation(ki_hi[r * ID:(r + 1) * ID, :], ps[0:ID, :], ACT.Copy).then_inc(ki_hi_done, 1)
                    elif kind == "qi":
                        act.wait_ge(bank_ready, n + 1)
                        act.activation(qi_hi[:, t, :], ps[:, :], ACT.Copy).then_inc(qi_hi_done, 1)
                        if t == 1:
                            act.wait_ge(t_ready, WI_TURN + 1)
                            act.activation(wi[:, :], t_bank[:, 0:TB * IH], ACT.Copy).then_inc(t_read, 1)
                    elif kind in ("v", "vm"):
                        act.wait_ge(bank_ready, n + 1)
                        dst = (v if kind == "v" else vm)[:, 2 * t:2 * t + 2, half * COLS:(half + 1) * COLS]
                        act.activation(dst, ps[:, :].rearrange("p (b n) -> p b n", b=2), ACT.Copy)\
                           .then_inc(bank_read["act"], 1)
                    elif kind == "c":
                        act.wait_ge(bank_ready, n + 1)
                        if half == 1:
                            act.wait_ge(conv_done, t + 1)
                        act.activation(cbuf[:, t, :], ps[:, :], ACT.Copy).then_inc(bank_read["act"], 1)
                    elif kind[0] == "g":
                        g = {"a": 0, "m": 8, "y": 16}[kind[1]] + 2 * half + t
                        act.wait_ge(bank_ready, n + 1)
                        if 4 <= g < 16:
                            act.wait_ge(t_used, g - 3)
                        act.activation(gate_slot(g), ps[:, :], ACT.Tanh, scale=0.5).then_inc(bank_read["act"], 1)
                    elif kind == "wy":
                        j = 4 * half + t
                        act.wait_ge(merged_done, j + 1)
                        act.activation(xn_hi[:, j, :], merged[:, j, :], ACT.Copy, scale=0.5).then_inc(mg_hi, 1)
                    if pending is not None:
                        chain_gain(pending)
                        pending = None
                    if kind in ("k", "q", "qm", "km"):
                        pending = chain_of[kind, half, t]
                    if kind in ("q", "v", "qm"):
                        for _ in range(2):
                            idx_relu(idx)
                            idx += 1
                    for s in slots_at.get((kind, half, t), ()):
                        slot(s)
                    if kind == "b":
                        act.wait_ge(bank_read["dve"], count(last_reader, "dve", n))
                        act.activation(ya_hi[:, 2 * half + t, :], cvbuf[:, t, :], ACT.Copy).then_inc(ya_hi_done, 1)
                if p < N_HEAD - 1:
                    split_head(p + 2)
                if kind == "qi":
                    for i in range(TB, TB + MB):
                        norm_sum(i)
            norm_his(TB + MB + 2, TB + MB + 3)

            def up(it):
                for q in range(4):
                    i = q % 2
                    act.wait_ge(bank_ready, it * 4 + (N_USES + q + 1))
                    act.wait_ge(pair_done, it * 2 + (i + 1))
                    act.activation(taps[:, q, :], banks[(N_USES + q) % 4][:, :], ACT.Copy,
                                   scale=cst[:, bass.ds(it * 2 + tap_f(2, (q // 2) * FT + i), 1)]).then_inc(tap_done, 1)
                    if i == 1:
                        act.wait_ge(raw_landed[q // 2], it * 16 + 16 * ((UP0 + q // 2 + 2) // 2 + 1))
                        split_hi(PANEL, q // 2)
                    if q == 1:
                        for g in range(2):
                            act.wait_ge(bank_read["dve"], it * 4 + (DVE_USES + g + 1))
                            act.activation(taps[:, g, :], taps[:, g, :], ACT.Silu).then_inc(silu_done, 1)

            def split_h_hi(d, slot):
                for c in range(2):
                    act.activation(xn_hi[:, 2 * slot + c, :], hraw[:, bass.ds(d * 2 + c, 1), :].squeeze(1),
                                   ACT.Copy).then_inc(h_hi, 1)

            up(0)
            act.wait_ge(pair_done, 4)
            split_h_hi(0, 0)
            with act.Fori(1, FT // 2) as it:
                up(it)
            act.wait_ge(pair_done, FT + 2)
            split_h_hi(1, 1)

            def down_next(d, slot):
                act.wait_ge(down_used, d + 1)
                act.wait_ge(raw_landed[slot], (d - slot) * 8 + 16 * (DOWN0 // 2 + 2))
                split_hi(PANEL, slot)
                split_h_hi(d + 2, slot)

            down_next(0, 0)
            with act.Fori(0, (N_DOWN - 3) // 2) as it:
                down_next(it * 2 + 1, 1)
                down_next(it * 2 + 2, 0)

        @block.vector
        def _(dve):
            steps = [0]

            def link(ins):
                steps[0] += 1
                ins.then_inc(dve_step, 1)
                dve.wait_ge(dve_step, steps[0])

            def split_lo(slot, n, hi_value, pieces=range(2)):
                for piece in pieces:
                    sl = slice(piece * n // 2, (piece + 1) * n // 2)
                    dve.wait_ge(hi_done, hi_value + (piece + 1))
                    dve.tensor_tensor(wlo[slot][:, sl], raw[slot][:, sl], whi[slot][:, sl], ALU.subtract)\
                       .then_inc(lo_done, 1)

            def split_head(p, pieces=range(2)):
                n = panels[p][2].shape[1] * panels[p][2].shape[2] if p < N_HEAD else PANEL
                split_lo(p % 2, n, 2 * p, pieces)

            def norm_mean(i):
                dve.wait_ge(n_sum, i + 1)
                kind, b = NORMS[i]
                if kind == "x2":
                    dve.scalar_tensor_tensor(n_ms[:, i:i + 1], n_ss[:, i:i + 1], 1.0 / D, n_ms1[:, b:b + 1],
                                             ALU.mult, ALU.add).then_inc(n_mean, 1)
                else:
                    dve.tensor_scalar(n_ms[:, i:i + 1], n_ss[:, i:i + 1], 1.0 / D, EPS, ALU.mult, ALU.add)\
                       .then_inc(n_mean, 1)

            def norm_scale(i):
                _, _, src, dst, *_ = norm_place(i)
                dve.wait_ge(n_rstd, i + 1)
                dve.tensor_scalar(dst, src, n_rs[:, i:i + 1], None, ALU.mult).then_inc(n_scaled, 1)

            def norm_gain(i, half):
                kind, b, _, _, hi, lo, tmp = norm_place(i)
                wait_turned(dve, i, half)
                if 2 * i + half >= 2:
                    dve.wait_ge(n_lo, 2 * i + half - 1)
                g0 = g_cols[kind] + 4 * half
                g = cst[:, g0:g0 + 4].unsqueeze(2).to_broadcast([P, 4, P])
                dve.tensor_tensor(tmp[half].rearrange("p (k t) -> p k t", k=4),
                                  norm_bank(i, half)[:, :].rearrange("p (k t) -> p k t", k=4), g,
                                  ALU.mult).then_inc(aside_gained if (i, half) in ASIDE else bank_read["dve"], 1)

            def norm_lo(i, half):
                _, b, _, _, hi, lo, tmp = norm_place(i)
                dve.wait_ge(n_hi, 2 * i + half + 1)
                at = (slice(None), slice(4 * half, 4 * half + 4), slice(b * P, (b + 1) * P))
                dve.tensor_tensor(lo[at], tmp[half].rearrange("p (k t) -> p k t", k=4), hi[at],
                                  ALU.subtract).then_inc(n_lo, 1)

            def norm_turned(*blocks):
                last = None
                for i in blocks:
                    for half in range(2):
                        norm_gain(i, half)
                        if last is not None:
                            norm_lo(*last)
                        last = (i, half)
                norm_lo(*last)

            def chain_stat(c):
                g, n = chain_shape(CHAINS[c][0])
                st = c_stats[:, c % 2, :]
                dve.wait_ge(c_sq, c + 1)
                link(dve.tensor_reduce(st[:, 0:n], sq[:, :].rearrange("p (n g) -> p n g", g=g), AX.X, ALU.add))
                dve.tensor_scalar(st[:, 8:8 + n], st[:, 0:n], 1.0 / g, EPS, ALU.mult, ALU.add).then_inc(c_mean, 1)

            def chain_norm(c, use):
                g, n = chain_shape(CHAINS[c][0])
                dve.wait_ge(c_rstd, c + 1)
                if c >= 2:
                    dve.wait_ge(t_ready, turn_of(c - 2) + 1)
                r = c_stats[:, c % 2, 16:16 + n].unsqueeze(2).to_broadcast([P, n, g])
                dve.tensor_tensor(qn[:, c % 2, :].rearrange("p (n g) -> p n g", g=g),
                                  banks[use % 4][:, :].rearrange("p (n g) -> p n g", g=g), r,
                                  ALU.mult).then_inc(bank_read["dve"], 1)

            def idx_add(u):
                b, h = IDX[u]
                n = (b + 1) * P
                sc = score[:, offset[b]:offset[b] + n]
                w = wi[:, b * IH + h:b * IH + h + 1]
                dve.wait_ge(s_read["act"], u + 1)
                if u == 0:
                    dve.wait_ge(t_read, WI_TURN + 1)
                if h == 0:
                    dve.tensor_scalar(sc, rl[:, u % 2, 0:n], w, 0.0, ALU.mult, ALU.add).then_inc(rl_used, 1)
                else:
                    dve.wait_ge(rl_used, u)
                    dve.scalar_tensor_tensor(sc, rl[:, u % 2, 0:n], w, sc, ALU.mult, ALU.add).then_inc(rl_used, 1)
                if h == IH - 1:
                    dve.wait_ge(rl_used, u + 1)
                    dve.wait_ge(pool_const, 6 + TB)
                    diag = score[:, offset[b] + b * P:offset[b] + n]
                    link(dve.tensor_tensor(diag, diag, causal[:, :], ALU.add))

            def topk_round(r):
                b, r = 1 + r // (TOPK // 8), r % (TOPK // 8)
                n = (b + 1) * P
                sc, wk = score[:, offset[b]:offset[b] + n], work[:, offset[b]:offset[b] + n]
                src = sc if r == 0 else wk
                link(dve.max(m8[:, :], src))
                link(dve.match_replace(wk, m8[:, :], src, FILL))
                if r == TOPK // 8 - 1:
                    link(dve.scalar_tensor_tensor(wk, wk, 1.0, sc, ALU.mult, ALU.is_equal))
                    link(dve.scalar_tensor_tensor(far[b][:, :], wk, FAR, far[b][:, :], ALU.mult, ALU.add))

            def topk_rounds(done, n):
                for r in range(done, done + n):
                    topk_round(r)
                return done + n

            def slot(s):
                if 0 <= s - 1 < N_UNITS:
                    u = s - 1
                    kind, h, b = UNITS[u]
                    pr = prob[:, u % 4, 0:keys(kind, b)]
                    dve.wait_ge(exp_done, u + 1)
                    link(dve.reciprocal(e_inv[:, u % 4:u % 4 + 1], e_sum[:, u % 4:u % 4 + 1]))
                    dve.tensor_scalar(pr, pr, e_inv[:, u % 4:u % 4 + 1], None, ALU.mult).then_inc(prob_done, 1)
                if s < N_UNITS:
                    kind, h, b = UNITS[s]
                    n = keys(kind, b)
                    dve.wait_ge(s_ready, len(IDX) + s + 1)
                    ps = s_bank[(len(IDX) + s) % 2][:, 0:n]
                    if kind == "s":
                        slope = 2.0 ** -(h + 1)
                        dve.wait_ge(t_ready, PT0 + s - 3)
                        dve.scalar_tensor_tensor(prob[:, s % 4, 0:n], far[b][:, :], -slope, ps, ALU.mult, ALU.add)\
                           .then_inc(s_read["dve"], 1)
                        dve.wait_ge(s_read["dve"], count(score_reader, "dve", len(IDX) + s))
                        ps = prob[:, s % 4, 0:n]
                    dve.tensor_reduce(e_max[:, s % 4:s % 4 + 1], ps, AX.X, ALU.max, negate=True).then_inc(max_done, 1)
                if s - 4 in group_end:
                    g = group_end[s - 4]
                    hi, lo = (ym_hi, ym_lo) if g < 4 else (yb_hi, yb_lo)
                    dve.wait_ge(o_hi, g + 1)
                    dve.tensor_tensor(lo[:, g % 4, :], o_bank[:, :], hi[:, g % 4, :], ALU.subtract).then_inc(o_lo, 1)

            norm_mean(0)
            norm_scale(0)
            split_lo(0, PANEL, 0, [0])
            dve.wait_ge(cst_ready, 1)
            link(dve.tensor_copy(cst[:, 0:G0 + 40], o_bank[:, 0:G0 + 40]))
            link(dve.tensor_scalar(cst[:, G0 + 40:G0 + 41], cst[:, G0 + 36:G0 + 37], HD ** -0.5, None, ALU.mult))
            dve.tensor_scalar(cst[:, G0 + 41:G0 + 42], cst[:, G0 + 38:G0 + 39], MHD ** -0.5, None, ALU.mult)\
               .then_inc(cst_done, 1)
            for i in range(TB):
                norm_gain(i, 0)
                norm_gain(i, 1)
                if i == 0:
                    norm_mean(1)
                norm_lo(i, 0)
                if i == 0:
                    norm_scale(1)
                    split_lo(0, PANEL, 0, [1])
                    norm_mean(2)
                    norm_mean(3)
                norm_lo(i, 1)

            idx, rounds = 0, 0
            for p, (kind, half, src) in enumerate(panels):
                for t in range(tiles_of(kind)[0] if kind != "wo" or half % 2 == 1 else 0):
                    n = use_of[kind, half - (kind == "wo"), t]
                    ps = banks[n % 4][:, :]
                    if (kind, half, t) in turned_in:
                        norm_gain(*turned_in[kind, half, t])
                    if kind in ("k", "q", "qm", "km"):
                        chain_stat(chain_of[kind, half, t])
                    if kind in ("q", "v", "qm"):
                        for _ in range(2):
                            idx_add(idx)
                            idx += 1
                    if (p, t) == (0, 0):
                        split_lo(1, PANEL, 2, [0])
                    if kind == "k" and t == 1:
                        split_head(p + 2, [0])
                    last = t == tiles_of(kind)[0] - 1
                    n_rounds = {"v": 2, "qm": 1, "km": 1, "vm": 2, "c": 2 if last else 4, "h": 1, "b": 1}.get(kind, 0)
                    if kind == "ga" and half < 2:
                        n_rounds = 2
                    if kind == "km" or kind in ("v", "qm") and not last:
                        rounds = topk_rounds(rounds, n_rounds)
                        n_rounds = 1 if kind == "km" else 0
                    if (kind, half, t) in turned_in:
                        norm_lo(*turned_in[kind, half, t])
                    if kind in ("k", "q", "qm", "km"):
                        chain_norm(chain_of[kind, half, t], n)
                        if (p, t) == (0, 0):
                            split_lo(1, PANEL, 2, [1])
                    elif kind == "ki":
                        dve.wait_ge(ki_hi_done, 4)
                        for r in range(4):
                            ins = dve.tensor_tensor(ki_lo[r * ID:(r + 1) * ID, :], ps[0:ID, :],
                                                    ki_hi[r * ID:(r + 1) * ID, :], ALU.subtract)
                            ins.then_inc(ki_lo_done if r < 3 else bank_read["dve"], 1)
                    elif kind == "qi":
                        dve.wait_ge(qi_hi_done, t + 1)
                        dve.tensor_tensor(qi_lo[:, t, :], ps, qi_hi[:, t, :], ALU.subtract).then_inc(bank_read["dve"], 1)
                    elif kind == "h":
                        u = cbuf[:, t, :]
                        dve.wait_ge(bank_ready, n + 1)
                        dve.wait_ge(bank_read["act"], count(last_reader, "act", use_of["c", half, t]))
                        dve.tensor_tensor(u, u, ps, ALU.mult).then_inc(bank_read["dve"], 1)
                    elif kind == "b":
                        j = 2 * half + t
                        cv = cvbuf[:, t, :]
                        dve.wait_ge(bank_ready, n + 1)
                        dve.wait_ge(conv_done, j + 1)
                        dve.tensor_tensor(cv, cv, ps, ALU.mult).then_inc(bank_read["dve"], 1)
                    elif kind[0] == "w" and kind != "wo":
                        g = {"a": 0, "m": 8, "y": 16}[kind[1]] + 4 * half + t
                        j = 4 * half + t
                        gt = gate_slot(g)
                        dve.wait_ge(bank_ready, n + 1)
                        dve.wait_ge(bank_read["act"], count(last_reader, "act",
                                                            use_of["g" + kind[1], 2 * half + t // 2, t % 2]))
                        mg = merged[:, j, :]
                        if kind == "wa":
                            dve.scalar_tensor_tensor(mg, gt, 1.0, ps, ALU.add, ALU.mult).then_inc(bank_read["dve"], 1)
                            dve.wait_ge(bank_read["dve"], count(last_reader, "dve", n))
                            dve.sem_inc(t_used, 1)
                        else:
                            dve.scalar_tensor_tensor(gt, gt, 1.0, ps, ALU.add, ALU.mult).then_inc(bank_read["dve"], 1)
                            dve.wait_ge(bank_read["dve"], count(last_reader, "dve", n))
                            done = t_used if kind == "wm" else merged_done
                            dve.tensor_tensor(mg, mg, gt, ALU.add).then_inc(done, 1)
                        if kind == "wy":
                            dve.wait_ge(mg_hi, j + 1)
                            dve.scalar_tensor_tensor(xn_lo[:, j, :], mg, 0.5, xn_hi[:, j, :], ALU.mult,
                                                     ALU.subtract).then_inc(mg_lo, 1)
                    elif kind == "wo":
                        i = TB + MB + t
                        if half == 3 and t == 3:
                            norm_turned(i - 2)
                        at = x2[:, t, (half // 2) * 512:(half // 2) * 512 + 512]
                        dve.wait_ge(bank_ready, n + 1)
                        dve.wait_ge(x2_landed, 16 * TB)
                        dve.tensor_tensor(at, at, ps, ALU.add).then_inc(bank_read["dve"], 1)
                        if half == 3:
                            if t == 2:
                                norm_gain(i - 2, 0)
                                norm_gain(i - 2, 1)
                            if t == 3:
                                split_lo((p + 2) % 2, PANEL, 2 * (p + 2), [0])
                            norm_mean(i)
                            if t == 3:
                                split_lo((p + 2) % 2, PANEL, 2 * (p + 2), [1])
                            if t == 2:
                                norm_lo(i - 2, 0)
                                norm_lo(i - 2, 1)
                    for s in slots_at.get((kind, half, t), ()):
                        slot(s)
                    if kind == "h":
                        j = 2 * half + t
                        u, cv = cbuf[:, t, :], cvbuf[:, t, :]
                        if half == 1:
                            dve.wait_ge(ya_lo_done, t + 1)
                        dve.wait_ge(bank_read["dve"], count(last_reader, "dve", n))
                        link(dve.tensor_scalar(cv, u, col(tap_a(2, j)), None, ALU.mult))
                        link(dve.scalar_tensor_tensor(cv[:, 1:T], u[:, 0:T - 1], col(tap_a(1, j)), cv[:, 1:T],
                                                      ALU.mult, ALU.add))
                        dve.scalar_tensor_tensor(cv[:, 2:T], u[:, 0:T - 2], col(tap_a(0, j)), cv[:, 2:T],
                                                 ALU.mult, ALU.add).then_inc(conv_done, 1)
                    elif kind == "b":
                        j = 2 * half + t
                        dve.wait_ge(ya_hi_done, j + 1)
                        dve.tensor_tensor(ya_lo[:, j, :], cvbuf[:, t, :], ya_hi[:, j, :], ALU.subtract)\
                           .then_inc(ya_lo_done, 1)
                    if not last:
                        rounds = topk_rounds(rounds, n_rounds)
                if kind == "wo" and half == 1:
                    dve.wait_ge(half_sum, TB)
                    link(dve.tensor_scalar(n_ms1, n_ss1, 1.0 / D, EPS, ALU.mult, ALU.add))
                if p < N_HEAD - 1:
                    split_head(p + 2, [1] if kind == "k" else range(2))
                if kind != "wo":
                    rounds = topk_rounds(rounds, n_rounds)
                if kind == "qi":
                    for i in range(TB, TB + MB):
                        norm_mean(i)
                        norm_scale(i)
            assert rounds == 3 * TOPK // 8 and idx == len(IDX)
            norm_turned(TB + MB + 2, TB + MB + 3)
            dve.wait_ge(n_lo, 2 * len(NORMS))
            dve.sem_inc(pair_done, 2)

            def up(it):
                def hidden(i):
                    dve.wait_ge(silu_done, it * 2 + (i + 1))
                    dve.wait_ge(bank_read["dve"], it * 4 + (DVE_USES + 3 + i))
                    dve.tensor_tensor(hraw[:, bass.ds(it * 2 + i, 1), :].squeeze(1), taps[:, i, :],
                                      taps[:, 2 + i, :], ALU.mult).then_inc(pair_done, 1)

                for q in range(4):
                    i = q % 2
                    tile = (q // 2) * FT + i
                    ps = banks[(N_USES + q) % 4]
                    dve.wait_ge(tap_done, it * 4 + (q + 1))
                    dve.scalar_tensor_tensor(taps[:, q, 1:T], ps[:, 0:T - 1], cst[:, bass.ds(it * 2 + tap_f(1, tile), 1)],
                                             taps[:, q, 1:T], ALU.mult, ALU.add).then_inc(tap_step, 1)
                    dve.wait_ge(tap_step, it * 4 + (q + 1))
                    dve.scalar_tensor_tensor(taps[:, q, 2:T], ps[:, 0:T - 2], cst[:, bass.ds(it * 2 + tap_f(0, tile), 1)],
                                             taps[:, q, 2:T], ALU.mult, ALU.add).then_inc(bank_read["dve"], 1)
                    if i == 1:
                        split_lo(q // 2, PANEL, it * 4 + 2 * (UP0 + q // 2 + 2))
                for i in range(2):
                    hidden(i)

            def split_h_lo(d, slot):
                for c in range(2):
                    dve.wait_ge(h_hi, d * 2 + (c + 1))
                    dve.tensor_tensor(xn_lo[:, 2 * slot + c, :], hraw[:, bass.ds(d * 2 + c, 1), :].squeeze(1),
                                      xn_hi[:, 2 * slot + c, :], ALU.subtract).then_inc(h_lo, 1)

            up(0)
            split_h_lo(0, 0)
            with dve.Fori(1, FT // 2) as it:
                up(it)
            split_h_lo(1, 1)

            def down_next(d, slot):
                split_lo(slot, PANEL, d * 2 + 2 * (DOWN0 + 2))
                split_h_lo(d + 2, slot)

            down_next(0, 0)
            with dve.Fori(0, (N_DOWN - 3) // 2) as it:
                down_next(it * 2 + 1, 1)
                down_next(it * 2 + 2, 0)
            for n in range(8):
                b, half = n // 2, n % 2
                at = x2[:, b, half * 512:half * 512 + 512]
                dve.wait_ge(bank_ready, N_USES + 2 * FT + n + 1)
                dve.tensor_tensor(at, at, banks[n][:, :], ALU.add).then_inc(out_done, 1)

        @block.tensor
        def _(pe):
            def product(o, a, b, start, stop):
                pe.matmul(o, a[0], b[0], start=start, stop=False)
                pe.matmul(o, a[0], b[1], start=False, stop=False)
                return pe.matmul(o, a[1], b[0], start=False, stop=stop)

            def bank_free(n):
                if n >= 4:
                    who = last_reader[n - 4]
                    pe.wait_ge(bank_read[who], count(last_reader, who, n - 4))

            def panel_there(p):
                pe.wait_ge(hi_done, p * 2 + 2)
                pe.wait_ge(lo_done, p * 2 + 2)

            def turn_norm(i, halves=range(2)):
                kind, b, _, dst, *_ = norm_place(i)
                pe.wait_ge(n_scaled, i + 1)
                for half in halves:
                    if (i, half) not in ASIDE:
                        bank_free(use_of["turn", i, half])
                    elif kind == "mem":
                        pe.wait_ge(cst_done, 1)
                        pe.wait_ge(aside_gained, ASIDE.index((i, half)))
                    elif (i, half) == (TB - 1, 1):
                        pe.wait_ge(cst_done, 1)
                    elif kind == "x2" and b >= 2:
                        pe.wait_ge(aside_gained, ASIDE.index((i, half)) - 3)
                    elif kind == "x2":
                        pe.wait_ge(s_read["dve"], score_reader.count("dve"))
                        pe.wait_ge(t_read, PT0 + N_UNITS)
                        pe.wait_ge(o_lo, 8)
                    for k in range(4):
                        c = (4 * half + k) * P
                        last = pe.transpose(norm_bank(i, half)[:, k * P:(k + 1) * P], dst[:, c:c + P], ident[:, :])
                    last.then_inc(aside_turned if (i, half) in ASIDE else bank_ready, 1)

            def turn_chain(c):
                n = use_of[CHAINS[c]]
                pe.wait_ge(bank_read["dve"], count(last_reader, "dve", n))
                pe.wait_ge(t_read, turn_of(c))
                if c == 0:
                    pe.wait_ge(aside_gained, ASIDE.index((TB - 1, 0)) + 1)
                for cc in range(2):
                    for bb in range(2):
                        last = pe.transpose(t_bank[:, (2 * cc + bb) * P:(2 * cc + bb + 1) * P],
                                            qn[:, c % 2, bb * COLS + cc * P:bb * COLS + (cc + 1) * P], ident[:, :])
                last.then_inc(t_ready, 1)

            def score_bank(k):
                if k >= 2:
                    who = score_reader[k - 2]
                    if who == "exp":
                        pe.wait_ge(exp_done, k - 1 - len(IDX))
                    else:
                        pe.wait_ge(s_read[who], count(score_reader, who, k - 2))
                return s_bank[k % 2]

            def idx_scores(u):
                b, h = IDX[u]
                r = (h % 4) * ID
                ps = score_bank(u)
                if u == 0:
                    pe.wait_ge(bank_read["dve"], count(last_reader, "dve", use_of["qi", 0, 1]))
                    pe.wait_ge(ki_lo_done, 3)
                product(ps[:, 0:(b + 1) * P], [a[r:r + ID, h // 4, b * P:(b + 1) * P] for a in (qi_hi, qi_lo)],
                        [a[r:r + ID, 0:(b + 1) * P] for a in (ki_hi, ki_lo)], True, True).then_inc(s_ready, 1)

            def slot(s):
                if s < N_UNITS:
                    kind, h, b = UNITS[s]
                    n = keys(kind, b)
                    ps = score_bank(len(IDX) + s)
                    if kind == "m":
                        lhs, rhs = qmT[:, h, b * P:(b + 1) * P], kmT[:, h, :]
                    else:
                        r = (h % 2) * HD
                        lhs, rhs = qT[r:r + HD, h // 2, b * P:(b + 1) * P], kT[r:r + HD, h // 2, 0:n]
                    if s == 0:
                        pe.wait_ge(t_read, PT0)
                    pe.matmul(ps[:, 0:n], lhs, rhs, start=True, stop=True).then_inc(s_ready, 1)
                if 0 <= s - 3 < N_UNITS:
                    u = s - 3
                    kind, h, b = UNITS[u]
                    pe.wait_ge(prob_done, u + 1)
                    pe.wait_ge(t_read, PT0 + u)
                    for j in range(keys(kind, b) // P):
                        last = pe.transpose(t_bank[:, j * P:(j + 1) * P], prob[:, u % 4, j * P:(j + 1) * P], ident[:, :])
                    last.then_inc(t_ready, 1)
                if 0 <= s - 4 < N_UNITS:
                    u = s - 4
                    kind, h, b = UNITS[u]
                    n = keys(kind, b) // P
                    pe.wait_ge(t_read, PT0 + u + 1)
                    if u in group_start and group_start[u] > 0:
                        pe.wait_ge(o_lo, group_start[u])
                    if u == 0:
                        pe.wait_ge(bank_read["act"], count(last_reader, "act", use_of["vm", 1, 0]))
                    for j in range(n):
                        if kind == "m":
                            o, lhs = o_bank[:, b * P:(b + 1) * P], vm[:, j, h * MHD:(h + 1) * MHD]
                        else:
                            r = (h % 2) * HD
                            o, lhs = o_bank[r:r + HD, b * P:(b + 1) * P], v[:, j, h * HD:(h + 1) * HD]
                        last = pe.matmul(o, lhs, probT[:, u % 2, j * P:(j + 1) * P], start=(j == 0), stop=(j == n - 1))
                    last.then_inc(o_ready, 1)

            def keep_clock(n):
                for _ in range(n):
                    pe.transpose(s_bank[1][:, 0:P], ident[:, :], ident[:, :])

            pe.wait_ge(pool_const, 2)
            keep_clock(22)
            turn_norm(0, (0,))
            pe.wait_ge(rows_landed, 16 * 5)
            pe.wait_ge(narrow_landed, 16 * 2)
            pe.wait_ge(wide_landed, 16 * 2)
            for tap in range(3):
                pe.transpose(o_bank[:, tap_f(tap, 0):tap_f(tap, 2 * FT)], stage_a[:, tap, :],
                             ident[0:2 * FT, 0:2 * FT])
            pe.transpose(o_bank[:, G0:G0 + 40], stage_b[:, :], ident[0:40, 0:40]).then_inc(cst_ready, 1)
            turn_norm(0, (1,))
            keep_clock(24)

            TURNS = {(0, 3): 1, (0, KD - 1): 2, (1, 2): 3}

            pending = None
            idx = 0
            for p, (kind, half, src) in enumerate(panels):
                k_in, cols = src.shape[1:]
                if kind == "km" and half == 0:
                    pe.wait_ge(n_lo, 2 * (TB + MB))
                w = small_panel(p % 2, k_in, cols)
                xn = (xn_hi, xn_lo)
                n_banks = tiles_of(kind)[0]
                for t in range(n_banks):
                    if t == 0 and kind != "k":
                        panel_there(p)
                    n = use_of[kind, half - half % 2 if kind == "wo" else half, t]
                    ps = banks[n % 4]
                    if kind != "wo" or half % 2 == 0:
                        bank_free(n)
                    if kind in ("k", "q", "v", "qm", "km", "vm"):
                        src_x = (memn_hi, memn_lo) if kind in ("km", "vm") else xn
                        for bb in range(2):
                            tok = slice((2 * t + bb) * P, (2 * t + bb + 1) * P)
                            for k in range(KD):
                                if kind == "k" and k % 4 == 0:
                                    pe.wait_ge(lo_done, 2 * p + k // 4 + 1)
                                    if half == 0:
                                        pe.wait_ge(n_lo, 2 * (2 * t + bb) + k // 4 + 1)
                                last = product(ps[:, bb * COLS:(bb + 1) * COLS], [a[:, k, tok] for a in src_x],
                                               [a[:, k, :] for a in w], k == 0, k == KD - 1)
                                if (p, t) == (0, 0) and (bb, k) in TURNS:
                                    turn_norm(TURNS[bb, k])
                            if bb == 0 and (kind, half, t) in turned_in:
                                i, h = turned_in[kind, half, t]
                                turn_norm(i, (h,))
                            if bb == 0 and kind in ("q", "v", "qm"):
                                idx_scores(idx)
                                idx += 1
                    elif kind == "wo":
                        kh = half % 2
                        if half < 2 and t == 0:
                            pe.wait_ge(mg_lo, 4 * (half + 1))
                        for k in range(4):
                            last = product(ps[:, :], [a[:, 4 * kh + k, t * P:(t + 1) * P] for a in xn],
                                           [a[:, k, :] for a in w], kh == 0 and k == 0, kh == 1 and k == 3)
                    elif kind[0] == "w":
                        y, there = {"wa": ((ya_hi, ya_lo), (ya_lo_done, 4)), "wm": ((ym_hi, ym_lo), (o_lo, 4)),
                                    "wy": ((yb_hi, yb_lo), (o_lo, 8))}[kind]
                        if kind != "wy":
                            pe.wait_ge(*there)
                        for k in range(4):
                            if kind == "wy":
                                pe.wait_ge(o_lo, 5 + k)
                            last = product(ps[:, :], [a[:, k, t * P:(t + 1) * P] for a in w],
                                           [a[:, k, :] for a in y], k == 0, k == 3)
                    else:
                        m = min(P, cols - t * P)
                        for k in range(KD):
                            last = product(ps[0:m, :], [a[:, k, t * P:t * P + m] for a in w],
                                           [a[:, k, :] for a in xn], k == 0, k == KD - 1)
                    if kind == "wo" and half % 2 == 0:
                        if t == n_banks - 1:
                            last.then_inc(wo_used, 1)
                    else:
                        last.then_inc(bank_ready, 1)
                    if kind == "wo" and half == 3 and t >= 2:
                        turn_norm(TB + MB + t - 2)
                        if t == 3:
                            turn_norm(TB + MB + 2)
                    if pending is not None:
                        turn_chain(pending)
                        pending = None
                    if kind in ("k", "q", "qm", "km"):
                        pending = chain_of[kind, half, t]
                    if kind == "qi" and t == 0:
                        pe.wait_ge(wiT_ready, 1)
                        pe.wait_ge(t_read, WI_TURN)
                        for b in range(TB):
                            last = pe.transpose(t_bank[:, b * IH:(b + 1) * IH], wiT[:, b * P:(b + 1) * P],
                                                ident[0:IH, 0:IH])
                        last.then_inc(t_ready, 1)
                    if kind in ("q", "v", "qm"):
                        idx_scores(idx)
                        idx += 1
                    for s in slots_at.get((kind, half, t), ()):
                        slot(s)

            def up_tile(q, tok, first=False):
                w = panel(q // 2, KD)
                for k in range(KD):
                    if first and k % 4 == 0:
                        pe.wait_ge(n_lo, 2 * (TB + MB + 1) + k // 4 + 1)
                    last = product(banks[(N_USES + q) % 4][:, tok], [a[:, k, (q % 2) * P:(q % 2 + 1) * P] for a in w],
                                   [xn2_hi[:, k, tok], xn2_lo[:, k, tok]], k == 0, k == KD - 1)
                return last

            for q in range(4):
                if q == 2:
                    turn_norm(len(NORMS) - 1)
                if q % 2 == 0:
                    panel_there(UP0 + q // 2)
                pe.wait_ge(bank_read["dve"], DVE_USES - 3 + q)
                up_tile(q, slice(0, T // 2), first=q == 0)
            pe.wait_ge(n_lo, 2 * len(NORMS))
            for q in range(4):
                up_tile(q, slice(T // 2, T)).then_inc(bank_ready, 1)
            with pe.Fori(1, FT // 2) as it:
                for q in range(4):
                    if q % 2 == 0:
                        panel_there(it * 2 + (UP0 + q // 2))
                    pe.wait_ge(bank_read["dve"], it * 4 + (DVE_USES - 3 + q))
                    up_tile(q, slice(0, T)).then_inc(bank_ready, 1)

            def down(d, slot, start=False, stop=False):
                panel_there(d + DOWN0)
                pe.wait_ge(h_lo, d * 2 + 2)
                w = panel(slot, 2)
                ring = [(N_USES + q) % 4 for q in range(4)]
                for n in [4, 5, 6, 7] + ring if start else range(8):
                    if start and n in ring:
                        pe.wait_ge(bank_read["dve"], DVE_USES + 2 * FT - 3 + ring.index(n))
                    b, half = n // 2, n % 2
                    for c in range(2):
                        last = product(banks[n][:, :], [a[:, 2 * slot + c, b * P:(b + 1) * P] for a in (xn_hi, xn_lo)],
                                       [a[:, c, half * 512:half * 512 + 512] for a in w],
                                       start and c == 0, stop and c == 1)
                    if stop:
                        last.then_inc(bank_ready, 1)
                if not stop:
                    last.then_inc(down_used, 1)

            pe.wait_ge(aside_gained, len(ASIDE))
            down(0, 0, start=True)
            with pe.Fori(0, (N_DOWN - 3) // 2) as it:
                down(it * 2 + 1, 1)
                down(it * 2 + 2, 0)
            down(N_DOWN - 2, 1)
            down(N_DOWN - 1, 0, stop=True)


INPUTS = ["x", "mem", "g_mix", "w_in", "conv_a_w", "w_a_out", "q_norm_g", "k_norm_g", "w_b_out", "g_mem", "w_mem_kv",
          "mq_norm_g", "mk_norm_g", "w_m_out", "w_o", "g_ffn", "w_up", "conv_f_w", "w_down"]


def kernel(**inputs):
    import numpy as np
    import concourse.bacc as bacc
    from concourse.bass_utils import run_bass_kernel_spmd

    nc = bacc.Bacc("TRN2", target_bir_lowering=False, num_devices=1)
    arrays, args = {}, []
    for name in INPUTS:
        a = np.ascontiguousarray(inputs[name])
        arrays["in_" + name] = a
        args.append(nc.dram_tensor("in_" + name, a.shape, mybir.dt.from_np(a.dtype), kind="ExternalInput").ap())
    args.append(nc.dram_tensor("layer_out", (1, T, D), F32, kind="ExternalOutput").ap())
    hybrid_layer(nc, *args)
    return run_bass_kernel_spmd(nc, [arrays], core_ids=[0]).results[0]["layer_out"]
```
